# Optimizing a Trainium2 kernel written in Bass

```python
import math
import jax, jax.numpy as jnp
from jax import lax
import numpy as np

D_MODEL = 2048
BATCH = 1
SEQ = 512
DEPTH = 2

CHUNK = 64
Q_BLOCK = 2 * CHUNK

N_A = (DEPTH + 1) // 2
N_B = DEPTH - N_A

D_RNN = 5 * D_MODEL // 4
LRU_BLOCKS = 10
LRU_BW = D_RNN // LRU_BLOCKS
CONV_W = 4
LRU_C = 8.0

N_HEADS = 16
HEAD_DIM = 128
D_ATTN = N_HEADS * HEAD_DIM

EPS = 1e-6

kernel_name = "hawk_stickbreak_yoco_trunk"

def _rmsnorm(x, g):
    xf = x.astype(jnp.float32)
    y = xf * lax.rsqrt(jnp.mean(xf * xf, axis=-1, keepdims=True) + EPS)
    return (y * g.astype(jnp.float32)).astype(x.dtype)

def _causal_depthwise_conv(xb, w, b):
    kernel = w[:, None, :].astype(xb.dtype)
    y = lax.conv_general_dilated(
        xb, kernel, window_strides=(1,), padding=[(CONV_W - 1, 0)],
        dimension_numbers=("NWC", "WIO", "NWC"), feature_group_count=xb.shape[-1])
    return y + b.astype(xb.dtype)

def _block_diag(xb, w, b):
    bsz, s, _ = xb.shape
    xr = xb.reshape(bsz, s, LRU_BLOCKS, LRU_BW)
    y = jnp.einsum("bsnc,ncd->bsnd", xr, w.astype(xb.dtype)).reshape(bsz, s, D_RNN)
    return y + b.astype(xb.dtype)

def _rg_lru(xb, w_r, b_r, w_i, b_i, lam):
    r = jax.nn.sigmoid(_block_diag(xb, w_r, b_r).astype(jnp.float32))
    i = jax.nn.sigmoid(_block_diag(xb, w_i, b_i).astype(jnp.float32))
    log_a = -LRU_C * r * jax.nn.softplus(-lam.astype(jnp.float32))
    a = jnp.exp(log_a)
    mult = jnp.sqrt(jnp.maximum(-jnp.expm1(2.0 * log_a), 0.0))
    u = mult * (i * xb.astype(jnp.float32))

    def combine(left, right):
        a1, b1 = left
        a2, b2 = right
        return a1 * a2, a2 * b1 + b2

    _, h = lax.associative_scan(combine, (a, u), axis=1)
    return h.astype(xb.dtype)

def _stick_breaking_attention(q, k, v):
    bsz, s, h, dh = q.shape
    n_blocks = s // Q_BLOCK
    scale = 1.0 / math.sqrt(dh)
    qb = q.reshape(bsz, n_blocks, Q_BLOCK, h, dh).transpose(1, 0, 2, 3, 4)
    starts = jnp.arange(n_blocks, dtype=jnp.int32) * Q_BLOCK
    key_pos = jnp.arange(s, dtype=jnp.int32)

    def one_block(args):
        start, qblk = args
        z = jnp.einsum("bqhd,bkhd->bhqk", qblk, k).astype(jnp.float32) * scale
        q_pos = start + jnp.arange(Q_BLOCK, dtype=jnp.int32)
        causal = key_pos[None, :] < q_pos[:, None]
        log_keep = jnp.where(causal, jax.nn.log_sigmoid(-z), 0.0)
        later = lax.cumsum(log_keep, axis=3, reverse=True) - log_keep
        weights = jnp.where(causal, jnp.exp(jax.nn.log_sigmoid(z) + later), 0.0)
        return jnp.einsum("bhqk,bkhd->bqhd", weights.astype(v.dtype), v)

    out = lax.map(one_block, (starts, qb))
    return out.transpose(1, 0, 2, 3, 4).reshape(bsz, s, h, dh)

def setup_inputs(seed: int = 0) -> dict:
    key = jax.random.key(seed)
    ks = jax.random.split(key, 20)

    def nrm(k, shape, scale):
        return jax.random.normal(k, shape, jnp.float32) * scale

    x = nrm(ks[0], (BATCH, SEQ, D_MODEL), 1.0)
    a_norm = 1.0 + nrm(ks[1], (N_A, D_MODEL), 0.01)
    a_w_in = nrm(ks[2], (N_A, D_MODEL, 2 * D_RNN), D_MODEL ** -0.5)
    a_conv_w = nrm(ks[3], (N_A, CONV_W, D_RNN), CONV_W ** -0.5)
    a_conv_b = nrm(ks[4], (N_A, D_RNN), 0.01)
    a_w_r = nrm(ks[5], (N_A, LRU_BLOCKS, LRU_BW, LRU_BW), LRU_BW ** -0.5)
    a_b_r = nrm(ks[6], (N_A, D_RNN), 0.01)
    a_w_i = nrm(ks[7], (N_A, LRU_BLOCKS, LRU_BW, LRU_BW), LRU_BW ** -0.5)
    a_b_i = nrm(ks[8], (N_A, D_RNN), 0.01)
    u = jax.random.uniform(ks[9], (N_A, D_RNN), jnp.float32, minval=0.9, maxval=0.999)
    a_root = u ** (1.0 / LRU_C)
    a_lambda = jnp.log(a_root) - jnp.log1p(-a_root)
    a_w_out = nrm(ks[10], (N_A, D_RNN, D_MODEL), D_RNN ** -0.5)
    kv_norm = 1.0 + nrm(ks[11], (D_MODEL,), 0.01)
    w_kv = nrm(ks[12], (D_MODEL, 2 * D_ATTN), D_MODEL ** -0.5)
    b_norm = 1.0 + nrm(ks[13], (N_B, D_MODEL), 0.01)
    b_w_in = nrm(ks[14], (N_B, D_MODEL, 2 * D_ATTN), D_MODEL ** -0.5)
    b_w_out = nrm(ks[15], (N_B, D_ATTN, D_MODEL), D_ATTN ** -0.5)
    final_norm = 1.0 + nrm(ks[16], (D_MODEL,), 0.01)
    return {
        "x": x, "a_norm": a_norm, "a_w_in": a_w_in, "a_conv_w": a_conv_w,
        "a_conv_b": a_conv_b, "a_w_r": a_w_r, "a_b_r": a_b_r, "a_w_i": a_w_i,
        "a_b_i": a_b_i, "a_lambda": a_lambda, "a_w_out": a_w_out,
        "kv_norm": kv_norm, "w_kv": w_kv, "b_norm": b_norm, "b_w_in": b_w_in,
        "b_w_out": b_w_out, "final_norm": final_norm,
    }

def reference(x, a_norm, a_w_in, a_conv_w, a_conv_b, a_w_r, a_b_r, a_w_i, a_b_i,
              a_lambda, a_w_out, kv_norm, w_kv, b_norm, b_w_in, b_w_out, final_norm):
    bsz, s, _ = x.shape
    k = v = None
    for layer in range(DEPTH):
        if layer < N_A:
            h = _rmsnorm(x, a_norm[layer])
            proj = h @ a_w_in[layer].astype(x.dtype)
            xb, gate = proj[..., :D_RNN], proj[..., D_RNN:]
            xb = _causal_depthwise_conv(xb, a_conv_w[layer], a_conv_b[layer])
            y = _rg_lru(xb, a_w_r[layer], a_b_r[layer], a_w_i[layer], a_b_i[layer],
                        a_lambda[layer])
            x = x + (y * jax.nn.silu(gate)) @ a_w_out[layer].astype(x.dtype)
            if layer == N_A - 1:
                kv = _rmsnorm(x, kv_norm) @ w_kv.astype(x.dtype)
                k = kv[..., :D_ATTN].reshape(bsz, s, N_HEADS, HEAD_DIM)
                v = kv[..., D_ATTN:].reshape(bsz, s, N_HEADS, HEAD_DIM)
        else:
            lb = layer - N_A
            h = _rmsnorm(x, b_norm[lb])
            proj = h @ b_w_in[lb].astype(x.dtype)
            q = proj[..., :D_ATTN].reshape(bsz, s, N_HEADS, HEAD_DIM)
            gate = proj[..., D_ATTN:]
            o = _stick_breaking_attention(q, k, v).reshape(bsz, s, D_ATTN)
            x = x + (o * jax.nn.silu(gate)) @ b_w_out[lb].astype(x.dtype)
    return _rmsnorm(x, final_norm)


_drawn_inputs = setup_inputs


def setup_inputs(seed=0):
    import zlib

    import numpy as np

    out = dict(_drawn_inputs(seed))
    spreads = {}
    factors = {'a_norm': 8.0,
     'a_b_r': 8.0,
     'a_b_i': 8.0,
     'kv_norm': 8.0,
     'b_norm': 8.0,
     'final_norm': 5.808}
    for name, (base, spread) in spreads.items():
        noise = np.random.default_rng([zlib.crc32(name.encode()), seed]).standard_normal(out[name].shape)
        drawn = base * np.exp(spread * noise) if base else spread * noise
        out[name] = __import__('jax').numpy.asarray(drawn.astype(out[name].dtype))
    for name, factor in factors.items():
        out[name] = (out[name] * factor).astype(out[name].dtype)
    return out
```

```python
from contextlib import ExitStack

import concourse.bass as bass
from concourse import mybir

F32 = mybir.dt.float32
F32R = mybir.dt.float32r
ACT = mybir.ActivationFunctionType
ALU = mybir.AluOpType
AX = mybir.AxisListType

P = 128
S = 512
D = 2048
R = 2560
KD = D // P
KR = R // P
TT = S // P
HEADS = 16
PAIRS = HEADS // 2
BLOCKS = 10
TAPS = 4
EPS = 1e-6
LRU_C = 8.0
SCALE = float(P) ** -0.5
MASKED = -1e30

RING = 4
AHEAD = 12
LOOK = AHEAD - RING
N1, N2, N3, N4 = 36, 20, 32, 64
B1, B2, B3 = BLOCKS // 2, KD // 4, PAIRS
U1 = 0
U2 = U1 + N1 * B1
U3 = U2 + N2 * B2
U4 = U3 + N3 * B3
UEND = U4 + N4

C_CONV, C_CB, C_BR, C_BI, C_LAM, C_GA, C_GKV, C_GB = 0, 80, 100, 120, 140, 160, 176, 192
NC = 208
ROWS_A = 120

Z_AT = {3: (4, 0), 2: (5, 0), 0: (5, 384), 1: (6, 0)}
WT_AT = {0: (4, 0), 1: (5, 0), 3: (5, 384), 2: (6, 0)}
W_OFF = {0: 0, 1: 128, 2: 384, 3: 768}
K_OFF = {0: 0, 1: 129, 2: 386, 3: 771}
WT_OFF = {0: 0, 1: 512, 3: 896, 2: 1024}
BANK_COLS = ((4, 0, 512), (5, 512, 512), (6, 1024, 256))
I_ORDER = (3, 2, 0, 1)
LOG1P_TERMS = (1 / 17, 1 / 15, 1 / 13, 1 / 11, 1 / 9, 1 / 7, 1 / 5, 1 / 3)


def build(nc, x, a_norm, a_w_in, a_conv_w, a_conv_b, a_w_r, a_b_r, a_w_i, a_b_i, a_lambda, a_w_out,
          kv_norm, w_kv, b_norm, b_w_in, b_w_out, final_norm, out, rs_dram):
    with ExitStack() as ctx:
        def sb(name, shape, dt=F32, scope=ctx):
            return scope.enter_context(nc.sbuf_tensor(name, shape, dt))

        def sem(name):
            return ctx.enter_context(nc.semaphore(name))

        stage = sb("stage", [P, RING, 512])
        w_hi = sb("w_hi", [P, RING, 512], F32R)
        w_lo = sb("w_lo", [P, RING, 512], F32R)
        x_hi = sb("x_hi", [P, KD, S], F32R)
        x_lo = sb("x_lo", [P, KD, S], F32R)
        rb = sb("rb", [P, S])
        g_fin = sb("g_fin", [P, D])
        ident = sb("ident", [P, P])
        ident_r = sb("ident_r", [P, P], F32R)
        mask_r = sb("mask_r", [P, P], F32R)
        ones = sb("ones", [P, P])
        mask_f = sb("mask_f", [P, P])
        cT = sb("cT", [P, NC])
        lam = sb("lam", [P, 6, KR])
        c_pos = sb("c_pos", [P, KR])
        c_neg = sb("c_neg", [P, KR])
        ss = sb("ss", [P, TT])
        rs_tok = sb("rs_tok", [P, TT])
        small = sb("small", [P, 3, TT])
        ss4 = sb("ss4", [P, TT, 4])

        with ExitStack() as mem12:
            y_hi = sb("y_hi", [P, KR, S], F32R, mem12)
            y_lo = sb("y_lo", [P, KR, S], F32R, mem12)
            with ExitStack() as mem0:
                xraw = sb("xraw", [P, TT, D], F32, mem0)
                rows_a = sb("rows_a", [P, P], F32, mem0)
                rows_b = sb("rows_b", [P, P], F32, mem0)
            with ExitStack() as mem1:
                xbp = sb("xbp", [P, 2, S + 4], F32, mem1)
                xc = sb("xc", [P, 2, S], F32, mem1)
                xc_hi = sb("xc_hi", [P, 2, S], F32R, mem1)
                xc_lo = sb("xc_lo", [P, 2, S], F32R, mem1)
                gate = sb("gate", [P, 2, S], F32, mem1)
                rbuf = sb("rbuf", [P, 2, S], F32, mem1)
                tbuf = sb("tbuf", [P, 2, S], F32, mem1)
                abuf = sb("abuf", [P, 2, S], F32, mem1)
            with ExitStack() as mem2:
                x1 = sb("x1", [P, 2, S], F32, mem2)
                sq = sb("sq", [P, 2, S], F32, mem2)
                acc = sb("acc", [P, S], F32, mem2)
                nrm = sb("nrm", [P, 3, S], F32, mem2)
        with ExitStack() as mem34:
            o_hi = sb("o_hi", [P, HEADS, S], F32R, mem34)
            o_lo = sb("o_lo", [P, HEADS, S], F32R, mem34)
            with ExitStack() as mem3:
                q_hi = sb("q_hi", [P, 2, S], F32R, mem3)
                q_lo = sb("q_lo", [P, 2, S], F32R, mem3)
                k_hi = sb("k_hi", [P, 2, S], F32R, mem3)
                k_lo = sb("k_lo", [P, 2, S], F32R, mem3)
                v_hi = sb("v_hi", [P, TT, 2 * P], F32R, mem3)
                v_lo = sb("v_lo", [P, TT, 2 * P], F32R, mem3)
                sg = sb("sg", [P, 2, S], F32, mem3)
                kf = sb("kf", [P, 2, S], F32, mem3)
                keep = sb("keep", [P, 1284], F32, mem3)
                wgt = sb("wgt", [P, 1280], F32, mem3)
                wt_hi = sb("wt_hi", [P, 1280], F32R, mem3)
                wt_lo = sb("wt_lo", [P, 1280], F32R, mem3)
            with ExitStack() as mem4:
                x2 = sb("x2", [P, TT, D], F32, mem4)
                junk = sb("junk", [P, 2, S], F32, mem4)
        ib = xbp[:, :, 3:3 + S]

        ps = [ctx.enter_context(nc.psum_tensor(f"ps{b}", [P, S], F32)) for b in range(8)]

        x_in = [sem(f"x_in{c}") for c in range(4)]
        rows_in = sem("rows_in")
        g_fin_in = sem("g_fin_in")
        stage_full = [sem(f"stage_full{s}") for s in range(RING)]
        hi_ready = sem("hi_ready")
        lo_ready = sem("lo_ready")
        w_used = sem("w_used")
        id_made = sem("id_made")
        rows_turned = sem("rows_turned")
        table_ready = sem("table_ready")
        x_turned = sem("x_turned")
        x_hi_ready = sem("x_hi_ready")
        x_lo_ready = sem("x_lo_ready")
        lam_exp = sem("lam_exp")
        dve_small = sem("dve_small")
        small_step = sem("small_step")
        ss_ready = sem("ss_ready")
        sqrt_in = sem("sqrt_in")
        sqrt_out = sem("sqrt_out")
        rs_stored = sem("rs_stored")
        rs_saved = sem("rs_saved")
        rb_in = sem("rb_in")
        xb_taken = sem("xb_taken")
        conv_step = sem("conv_step")
        xc_hi_ready = sem("xc_hi_ready")
        xc_lo_ready = sem("xc_lo_ready")
        gate_taken = sem("gate_taken")
        gate_sig = sem("gate_sig")
        gate_ready = sem("gate_ready")
        ri_ready = sem("ri_ready")
        a_ready = sem("a_ready")
        a2_ready = sem("a2_ready")
        expm1_ready = sem("expm1_ready")
        ix_ready = sem("ix_ready")
        v_ready = sem("v_ready")
        m_ready = sem("m_ready")
        u_ready = sem("u_ready")
        h_ready = sem("h_ready")
        y_ready = sem("y_ready")
        y_hi_ready = sem("y_hi_ready")
        y_lo_ready = sem("y_lo_ready")
        res_step = sem("res_step")
        sq_ready = sem("sq_ready")
        x1_hi_ready = sem("x1_hi_ready")
        x1_lo_ready = sem("x1_lo_ready")
        acc_step = sem("acc_step")
        stat_ready = sem("stat_ready")
        norm2_ready = sem("norm2_ready")
        g_taken = sem("g_taken")
        g_sig = sem("g_sig")
        sg_ready = sem("sg_ready")
        qk_f = sem("qk_f")
        qk_hi_ready = sem("qk_hi_ready")
        qk_lo_ready = sem("qk_lo_ready")
        v_hi_ready = sem("v_hi_ready")
        v_lo_ready = sem("v_lo_ready")
        z_ready = sem("z_ready")
        sig_ready = sem("sig_ready")
        stick_ready = sem("stick_ready")
        wgt_ready = sem("wgt_ready")
        wt_turned = sem("wt_turned")
        wt_hi_ready = sem("wt_hi_ready")
        wt_lo_ready = sem("wt_lo_ready")
        pv_done = sem("pv_done")
        o_f = sem("o_f")
        o_hi_ready = sem("o_hi_ready")
        o_lo_ready = sem("o_lo_ready")
        x2_sq = sem("x2_sq")
        x2_taken = sem("x2_taken")
        scaled = [sem(f"scaled{t}") for t in range(TT)]
        stored = sem("stored")

        def f(ap):
            return ap.bitcast(F32)

        def gain_column(phase, j):
            if phase == 1:
                return C_GA + 2 * (j % 18 % 8) if j % 18 < 16 else None
            if phase == 3:
                return (C_GB if j // 8 < 2 else C_GKV) + 2 * (j % 8)
            return None

        def ahead(phase, n, last, q):
            u = q + AHEAD
            if u < n or not last:
                return phase, u % n, u
            return phase + 1, u - n, u

        block = ctx.enter_context(nc.Block())

        @block.sync
        def _(sp):
            def load(src, j, first, u):
                if not first:
                    sp.wait_ge(lo_ready, u - RING + 1)
                dst = stage[:, j % RING, :]
                if src.shape[0] == 2 * P:
                    dst = dst.rearrange("p (k c) -> p k c", k=2)
                    src = src.rearrange("(k p) c -> p k c", p=P)
                sp.dma_start(dst, src).then_inc(stage_full[j % RING], 16)

            def at(col, width=256):
                return bass.ds(col if isinstance(col, int) else sp.snap(col), width)

            def src1(n, j):
                j = j % 18
                if j >= 16:
                    w = a_w_r if j == 16 else a_w_i
                    return w[0, at(n, 1), :, :].rearrange("a r c -> (a r) c")
                return a_w_in[0, 256 * (j % 8):256 * (j % 8) + 256, at(n * 256 + (j // 8) * R)]

            def src3(p, j):
                w, half = ((b_w_in[0], 1), (b_w_in[0], 0), (w_kv, 0), (w_kv, 1))[j // 8]
                w = w.rearrange("r (n c) -> n r c", c=256)
                return w[at(p + half * PAIRS, 1), 256 * (j % 8):256 * (j % 8) + 256, :].rearrange("n r c -> (n r) c")

            for t, first, rows in (
                    (rows_a, 0, a_conv_w.rearrange("a k (t p) -> (a k t) p", p=P)),
                    (rows_a, 80, a_conv_b.rearrange("a (t p) -> (a t) p", p=P)),
                    (rows_a, 100, a_b_r.rearrange("a (t p) -> (a t) p", p=P)),
                    (rows_b, 0, a_b_i.rearrange("a (t p) -> (a t) p", p=P)),
                    (rows_b, 20, a_lambda.rearrange("a (t p) -> (a t) p", p=P)),
                    (rows_b, 40, a_norm.rearrange("a (t p) -> (a t) p", p=P)),
                    (rows_b, 56, kv_norm.rearrange("(t p) -> t p", p=P)),
                    (rows_b, 72, b_norm.rearrange("a (t p) -> (a t) p", p=P))):
                sp.dma_start(t[first:first + rows.shape[0], :], rows).then_inc(rows_in, 16)
            x_v = x.rearrange("b (t p) n -> p (b t) n", p=P)
            for c in range(4):
                sp.dma_start(xraw[:, :, 512 * c:512 * c + 512], x_v[:, :, 512 * c:512 * c + 512]).then_inc(x_in[c], 16)
                load(src1(0, c), c, True, c)
            for j in range(RING, N1):
                load(src1(j // 18, j), j, False, U1 + j)
                if j == 8:
                    sp.wait_ge(rs_stored, 1)
                    with nc.allow_non_contiguous_dma(reason="512 single numbers"):
                        sp.dma_start(rs_dram.rearrange("t p -> p t"), rs_tok[:, :]).then_inc(rs_saved, 16)
                    sp.wait_ge(rs_saved, 16)
                    row = rs_dram.rearrange("t p -> (t p)").rearrange("(a n) -> a n", a=1)
                    sp.dma_start(rb[:, :], row.to_broadcast([P, S])).then_inc(rb_in, 16)
                if j == 20:
                    g_row = final_norm.rearrange("(a n) -> a n", a=1)
                    sp.dma_start(g_fin[:, :], g_row.to_broadcast([P, D])).then_inc(g_fin_in, 16)
            with sp.Fori(1, B1) as it:
                for j in range(N1):
                    load(src1(it * 2 + j // 18, j), j, False, it * N1 + (U1 + j))
            with sp.Fori(0, B2) as it:
                for j in range(N2):
                    rows = 256 * (j % 10)
                    load(a_w_out[0, rows:rows + 256, at(it * 512 + 256 * (j // 10))], j, False,
                         it * N2 + (U2 + j))
            with sp.Fori(0, B3) as it:
                for j in range(N3):
                    load(src3(it, j), j, False, it * N3 + (U3 + j))
            for j in range(N4):
                k, c = j % KD, j // KD
                load(b_w_out[0, P * k:P * k + P, 512 * c:512 * c + 512], j, False, U4 + j)
            o_v = out.rearrange("b (t p) n -> (b t) p n", p=P)
            for t in range(TT):
                sp.wait_ge(scaled[t], 1)
                sp.dma_start(o_v[t], x2[:, t, :]).then_inc(stored, 16)
            sp.wait_ge(stored, 16 * TT)

        @block.tensor
        def _(pe):
            def product(dst, a_hi, a_lo, b_hi, b_lo, start, stop, check=True):
                for n, (a, b) in enumerate(((a_hi, b_hi), (a_hi, b_lo), (a_lo, b_hi))):
                    mm = pe.matmul(dst, a, b, start=start and n == 0, stop=stop and n == 2,
                                   skip_group_check=not check)
                return mm

            def unit_t(j, u, bank, m_hi, m_lo, k0, k_end):
                pe.wait_ge(lo_ready, u + 1)
                s = j % RING
                for kk in range(2):
                    for m in range(2):
                        c = 256 * kk + P * m
                        mm = product(ps[bank + m][:, :], w_hi[:, s, c:c + P], w_lo[:, s, c:c + P],
                                     m_hi[:, k0 + kk, :], m_lo[:, k0 + kk, :],
                                     k0 + kk == 0, k0 + kk == k_end - 1)
                mm.then_inc(w_used, 1)

            pe.wait_ge(id_made, 4)
            pe.wait_ge(rows_in, 16 * 8)
            pe.transpose(ps[0][:, 0:ROWS_A], rows_a[0:ROWS_A, :], ident[0:ROWS_A, 0:ROWS_A])
            pe.transpose(ps[0][:, ROWS_A:NC], rows_b[0:NC - ROWS_A, :],
                         ident[0:NC - ROWS_A, 0:NC - ROWS_A]).then_inc(rows_turned, 1)
            for k in range(KD):
                if k % 4 == 0:
                    pe.wait_ge(x_in[k // 4], 16)
                if k >= 4:
                    pe.wait_ge(x_lo_ready, k - 3)
                for t in range(TT):
                    mm = pe.transpose(ps[4 + k % 4][:, P * t:P * t + P], xraw[:, t, P * k:P * k + P], ident[:, :])
                mm.then_inc(x_turned, 1)

            with pe.Fori(0, B1) as it:
                for j in range(N1):
                    u = it * N1 + (U1 + j)
                    b, jj = j // 18, j % 18
                    if jj < 16:
                        if j < 8:
                            pe.wait_ge(x_lo_ready, 2 * j + 2)
                        unit_t(j, u, 2 * (jj // 8), x_hi, x_lo, 2 * (jj % 8), KD)
                    else:
                        if jj == 16:
                            pe.wait_ge(xc_lo_ready, it * 4 + 2 * b + 2)
                        unit_t(j, u, 4 + 2 * (jj - 16), xc_hi, xc_lo, 0, 2)

            with pe.Fori(0, B2) as it:
                for j in range(N2):
                    jj = j % 10
                    if j < 10:
                        pe.wait_ge(y_lo_ready, 1 + 2 * jj + 2)
                    unit_t(j, it * N2 + (U2 + j), 2 * (j // 10), y_hi, y_lo, 2 * jj, KR)

            def proj3(j, u):
                if j < 24:
                    unit_t(j, u, 2 * (j // 8 % 2), x_hi, x_lo, 2 * (j % 8), KD)
                    return
                pe.wait_ge(lo_ready, u + 1)
                s = j % RING
                for kk in range(2):
                    k = 2 * (j % 8) + kk
                    for t in range(TT):
                        mm = product(ps[2 + t // 2][:, 256 * (t % 2):256 * (t % 2) + 256],
                                     x_hi[:, k, P * t:P * t + P], x_lo[:, k, P * t:P * t + P],
                                     w_hi[:, s, 256 * kk:256 * kk + 256], w_lo[:, s, 256 * kk:256 * kk + 256],
                                     k == 0 and t % 2 == 0, k == KD - 1, check=False)
                mm.then_inc(w_used, 1)

            def scores(p, h):
                pe.wait_ge(qk_lo_ready, p * 4 + 4)
                if h == 1:
                    pe.wait_ge(wt_lo_ready, p * 6 + 3)
                for i in I_ORDER:
                    bank, c = Z_AT[i]
                    n = P * (i + 1)
                    product(ps[bank][:, c:c + n], q_hi[:, h, P * i:P * i + P], q_lo[:, h, P * i:P * i + P],
                            k_hi[:, h, 0:n], k_lo[:, h, 0:n], True, False, check=False)
                    mm = pe.matmul(ps[bank][:, c + n - P:c + n], ident_r[:, :], mask_r[:, :],
                                   start=False, stop=True, skip_group_check=True)
                    if i != 2:
                        mm.then_inc(z_ready, 1)

            def turn_weights(p, h):
                pe.wait_ge(wgt_ready, p * 8 + (4 * h + 4))
                for k in (0, 1, 3, 2):
                    bank, c = WT_AT[k]
                    for i in range(k, TT):
                        mm = pe.transpose(ps[bank][:, c + P * (i - k):c + P * (i - k) + P],
                                          wgt[:, W_OFF[i] + P * k:W_OFF[i] + P * k + P], ident[:, :])
                    if k != 1:
                        mm.then_inc(wt_turned, 1)

            def values(p, h):
                pe.wait_ge(wt_lo_ready, p * 6 + (3 * h + 3))
                pe.wait_ge(v_lo_ready, p * 4 + 4)
                if h == 1:
                    pe.wait_ge(o_f, p * 2 + 1)
                for k in range(TT):
                    a, n = WT_OFF[k], S - P * k
                    mm = product(ps[7][:, P * k:S], v_hi[:, k, P * h:P * h + P], v_lo[:, k, P * h:P * h + P],
                                 wt_hi[:, a:a + n], wt_lo[:, a:a + n], k == 0, k == TT - 1, check=False)
                mm.then_inc(pv_done, 1)

            for j in range(8):
                pe.wait_ge(x1_lo_ready, 2 * j + 2)
                if j == 6:
                    pe.wait_ge(acc_step, 2 + KD)
                    pe.matmul(ps[4][:, :], ones[:, :], acc[:, :], start=True, stop=True).then_inc(stat_ready, 1)
                    for t in range(TT):
                        mm = pe.matmul(ps[5][:, t:t + 1], acc[:, P * t:P * t + P], ones[:, 0:1],
                                       start=True, stop=True)
                    mm.then_inc(stat_ready, 1)
                proj3(j, U3 + j)

            def pair_rest(p, next_unit):
                for j in range(8, 40):
                    if j == 26:
                        scores(p, 0)
                    if j == 30:
                        turn_weights(p, 0)
                    if j == 32:
                        scores(p, 1)
                    if j == 34:
                        values(p, 0)
                    if j == 36:
                        turn_weights(p, 1)
                    if j == 38:
                        values(p, 1)
                    if j < 32:
                        proj3(j, p * N3 + (U3 + j))
                    else:
                        next_unit(j - 32)

            with pe.Fori(0, B3 - 1) as it:
                pair_rest(it, lambda j: proj3(j, it * N3 + (U3 + N3 + j)))

            def unit4(j):
                k, c = j % KD, j // KD
                if c == 0:
                    pe.wait_ge(o_lo_ready, 1 + k + 1)
                if j == 0:
                    pe.wait_ge(v_lo_ready, 4 * PAIRS)
                pe.wait_ge(lo_ready, U4 + j + 1)
                s = j % RING
                for t in range(TT):
                    bank = ps[4 * (c % 2) + t]
                    mm = product(bank[:, :], o_hi[:, k, P * t:P * t + P], o_lo[:, k, P * t:P * t + P],
                                 w_hi[:, s, :], w_lo[:, s, :], k == 0, False, check=False)
                    if k == KD - 1:
                        for n in range(4):
                            for part in (x_lo, x_hi):
                                mm = pe.matmul(bank[:, P * n:P * n + P], part[:, 4 * c + n, P * t:P * t + P],
                                               ident_r[:, :], start=False, stop=part is x_hi and n == 3,
                                               skip_group_check=True)
                mm.then_inc(w_used, 1)

            pair_rest(B3 - 1, unit4)
            for j in range(8, N4):
                unit4(j)

        @block.scalar
        def _(act):
            def split_hi(phase, j, slot):
                col = gain_column(phase, j)
                if col is None:
                    nc.scalar.activation(w_hi[:, slot, :], stage[:, slot, :], ACT.Copy).then_inc(hi_ready, 1)
                    return
                nc.scalar.activation(w_hi[:, slot, 0:256], stage[:, slot, 0:256], ACT.Identity,
                                     scale=cT[:, col:col + 1])
                nc.scalar.activation(w_hi[:, slot, 256:512], stage[:, slot, 256:512], ACT.Identity,
                                     scale=cT[:, col + 1:col + 2]).then_inc(hi_ready, 1)

            def hi(phase, j, u):
                act.wait_ge(stage_full[u % RING], 16 * (u // RING + 1))
                if u >= RING:
                    act.wait_ge(w_used, u - RING + 1)
                split_hi(phase, j, u % RING)

            def hi_at(phase, n, base, it, last, q):
                ph, j, off = ahead(phase, n, last, q)
                slot = off % RING
                first = base + off - slot
                act.wait_ge(stage_full[slot], it * (4 * n) + (4 * first + 16))
                act.wait_ge(w_used, it * n + (base + off - RING + 1))
                split_hi(ph, j, slot)

            act.wait_ge(table_ready, 1)
            for j in range(RING):
                hi(1, j, U1 + j)
            for k in range(KD):
                act.wait_ge(x_turned, k + 1)
                nc.scalar.copy(x_hi[:, k, :], ps[4 + k % 4][:, :]).then_inc(x_hi_ready, 1)
            act.wait_ge(lam_exp, 1)
            nc.scalar.activation(lam[:, 1, :], lam[:, 0, :], ACT.Exp, scale=-1.0).then_inc(lam_exp, 1)
            for t in range(TT):
                nc.scalar.activation(xraw[:, t, :], xraw[:, t, :], ACT.Square,
                                     accum_out=ss[:, t:t + 1]).then_inc(ss_ready, 1)
            act.wait_ge(sqrt_in, 1)
            nc.scalar.activation(small[:, 1, :], small[:, 1, :], ACT.Sqrt).then_inc(sqrt_out, 1)
            for j in range(RING, AHEAD):
                hi(1, j, U1 + j)

            def work1(it, pos):
                b = 1 if pos >= 26 else 0
                rel = pos - 18 * b
                if rel == 11:
                    for m in range(2):
                        act.wait_ge(conv_step, it * 16 + (8 * b + 7 + m))
                        nc.scalar.copy(xc_hi[:, m, :], xc[:, m, :]).then_inc(xc_hi_ready, 1)
                if rel == 16:
                    for m in range(2):
                        act.wait_ge(gate_taken, it * 4 + (2 * b + m + 1))
                        nc.scalar.activation(rbuf[:, m, :], gate[:, m, :], ACT.Sigmoid).then_inc(gate_sig, 1)
                if pos in range(18, 26) or pos in range(36, 44):
                    b = (pos - 18) // 18
                    rel = (pos - 18) % 18
                    t0 = it * 4 + 2 * b
                    if rel == 0:
                        act.wait_ge(w_used, it * N1 + (U1 + 18 * b + 18))
                        for m in range(2):
                            act.wait_ge(gate_ready, it * 4 + (2 * b + m + 1))
                            nc.scalar.activation(rbuf[:, m, :], ps[4 + m][:, :], ACT.Sigmoid,
                                                 bias=cT[:, bass.ds(t0 + (C_BR + m), 1)]).then_inc(ri_ready, 1)
                        for m in range(2):
                            nc.scalar.activation(ib[:, m, :], ps[6 + m][:, :], ACT.Sigmoid,
                                                 bias=cT[:, bass.ds(t0 + (C_BI + m), 1)]).then_inc(ri_ready, 1)
                    if rel == 1:
                        for m in range(2):
                            act.wait_ge(ri_ready, it * 8 + (4 * b + m + 1))
                            nc.scalar.activation(tbuf[:, m, :], rbuf[:, m, :], ACT.Tanh,
                                                 scale=c_pos[:, bass.ds(t0 + m, 1)])
                        for m in range(2):
                            nc.scalar.activation(abuf[:, m, :], rbuf[:, m, :], ACT.Exp,
                                                 scale=c_neg[:, bass.ds(t0 + m, 1)]).then_inc(a_ready, 1)
                        for m in range(2):
                            act.wait_ge(a_ready, it * 4 + (2 * b + m + 1))
                            nc.scalar.activation(rbuf[:, m, :], abuf[:, m, :], ACT.Square).then_inc(a2_ready, 1)
                    if rel == 3:
                        for m in range(2):
                            act.wait_ge(v_ready, it * 4 + (2 * b + m + 1))
                            nc.scalar.activation(tbuf[:, m, :], tbuf[:, m, :], ACT.Sqrt).then_inc(m_ready, 1)
                    if rel == 6:
                        for m in range(2):
                            act.wait_ge(y_ready, it * 4 + (2 * b + m + 1))
                            nc.scalar.copy(y_hi[:, bass.ds(t0 + m, 1), :],
                                           gate[:, m:m + 1, :]).then_inc(y_hi_ready, 1)

            def body1(it, last):
                for q in range(N1):
                    hi_at(1, N1, U1, it, last, q)
                    work1(it, q + LOOK)

            with act.Fori(0, B1 - 1) as it:
                body1(it, False)
            body1(B1 - 1, True)

            def work2(it, pos):
                for b in range(2):
                    if pos == 10 * b + 11:
                        for m in range(2):
                            act.wait_ge(res_step, it * 8 + (4 * b + m + 3))
                            act.wait_ge(acc_step, it * 4 + (2 * b + m + 1))
                            nc.scalar.activation(sq[:, m, :], x1[:, m, :], ACT.Square).then_inc(sq_ready, 1)
                            nc.scalar.copy(x_hi[:, bass.ds(it * 4 + (2 * b + m), 1), :],
                                           x1[:, m:m + 1, :]).then_inc(x1_hi_ready, 1)

            def body2(it, last):
                for q in range(N2):
                    hi_at(2, N2, U2, it, last, q)
                    work2(it, q + LOOK)
                    if last and q + LOOK == 26:
                        act.wait_ge(sqrt_in, 2)
                        nc.scalar.activation(nrm[:, 1, :], nrm[:, 1, :], ACT.Sqrt).then_inc(sqrt_out, 1)
                        act.wait_ge(sqrt_in, 3)
                        nc.scalar.activation(small[:, 1, :], small[:, 1, :], ACT.Sqrt).then_inc(sqrt_out, 1)

            with act.Fori(0, B2 - 1) as it:
                body2(it, False)
            body2(B2 - 1, True)

            def sticks(p, h, tiles):
                for i in tiles:
                    bank, c = Z_AT[i]
                    n = P * (i + 1)
                    act.wait_ge(z_ready, p * 6 + (3 * h + bank - 3))
                    nc.scalar.activation(keep[:, K_OFF[i]:K_OFF[i] + n], ps[bank][:, c:c + n], ACT.Sigmoid,
                                         scale=-SCALE).then_inc(sig_ready, 1)
                    nc.scalar.activation(wgt[:, W_OFF[i]:W_OFF[i] + n], ps[bank][:, c:c + n], ACT.Sigmoid,
                                         scale=SCALE).then_inc(sig_ready, 1)

            def turned_hi(p, h):
                for n, (bank, a, w) in enumerate(BANK_COLS):
                    act.wait_ge(wt_turned, p * 6 + (3 * h + n + 1))
                    nc.scalar.copy(wt_hi[:, a:a + w], ps[bank][:, 0:w]).then_inc(wt_hi_ready, 1)

            def out_hi(p, h):
                act.wait_ge(o_f, p * 2 + (h + 1))
                nc.scalar.copy(o_hi[:, bass.ds(p * 2 + h, 1), :], kf[:, h:h + 1, :]).then_inc(o_hi_ready, 1)

            def work3(p, pos):
                if pos == 8:
                    for m in range(2):
                        act.wait_ge(g_taken, p * 2 + (m + 1))
                        act.wait_ge(o_lo_ready, p * 2 + 1)
                        nc.scalar.activation(kf[:, m, :], sg[:, m, :], ACT.Sigmoid).then_inc(g_sig, 1)
                for at, (dst, c) in ((16, (q_hi, 0)), (24, (k_hi, 2))):
                    if pos == at:
                        for m in range(2):
                            act.wait_ge(qk_f, p * 4 + (c + m + 1))
                            nc.scalar.copy(dst[:, m, :], kf[:, m, :]).then_inc(qk_hi_ready, 1)
                if pos == 31:
                    act.wait_ge(w_used, p * N3 + (U3 + N3))
                    for t in range(TT):
                        nc.scalar.activation(v_hi[:, t, :], ps[2 + t // 2][:, 256 * (t % 2):256 * (t % 2) + 256],
                                             ACT.Identity, scale=rs_tok[:, t:t + 1]).then_inc(v_hi_ready, 1)
                if pos in (26, 32):
                    sticks(p, pos // 32, (3, 2))
                if pos in (27, 33):
                    sticks(p, pos // 32, (0, 1))
                if pos in (30, 36):
                    turned_hi(p, pos // 36)
                if pos in (34, 38):
                    out_hi(p, pos // 38)

            def body3(p, last):
                for q in range(N3):
                    hi_at(3, N3, U3, p, last, q)
                    work3(p, q + LOOK)

            with act.Fori(0, B3 - 1) as it:
                body3(it, False)
            body3(B3 - 1, True)

            def squares(c):
                for t in range(TT):
                    if c == 3:
                        act.wait_ge(w_used, UEND)
                    if c or t >= 2:
                        act.wait_ge(x2_sq, TT * c + t - 1)
                    nc.scalar.activation(junk[:, t % 2, :], ps[4 * (c % 2) + t][:, :], ACT.Square,
                                         accum_out=ss4[:, t, c:c + 1]).then_inc(x2_sq, 1)

            for u in range(AHEAD, N4):
                hi(4, u, U4 + u)
                if u - RING in (16, 32, 48):
                    squares((u - RING) // 16 - 1)
            squares(3)
            act.wait_ge(sqrt_in, 4)
            nc.scalar.activation(small[:, 1, :], small[:, 1, :], ACT.Sqrt).then_inc(sqrt_out, 1)
            act.wait_ge(small_step, 1)
            for t in (0, 2):
                nc.scalar.activation(x2[:, t, :], x2[:, t, :], ACT.Identity,
                                     scale=rs_tok[:, t:t + 1]).then_inc(scaled[t], 1)

        @block.vector
        def _(dve):
            own = [0]

            def link(ins):
                own[0] += 1
                ins.then_inc(dve_small, 1)
                dve.wait_ge(dve_small, own[0])

            def lo(phase, j, slot, u):
                dve.wait_ge(hi_ready, u + 1)
                col = gain_column(phase, j)
                if col is None:
                    nc.vector.tensor_tensor(w_lo[:, slot, :], stage[:, slot, :], f(w_hi[:, slot, :]),
                                            ALU.subtract).then_inc(lo_ready, 1)
                    return
                nc.vector.scalar_tensor_tensor(w_lo[:, slot, 0:256], stage[:, slot, 0:256], cT[:, col:col + 1],
                                               f(w_hi[:, slot, 0:256]), ALU.mult, ALU.subtract)
                nc.vector.scalar_tensor_tensor(w_lo[:, slot, 256:512], stage[:, slot, 256:512],
                                               cT[:, col + 1:col + 2], f(w_hi[:, slot, 256:512]),
                                               ALU.mult, ALU.subtract).then_inc(lo_ready, 1)

            def lo_at(phase, n, base, it, last, q):
                ph, j, off = ahead(phase, n, last, q)
                lo(ph, j, off % RING, it * n + (base + off))

            def rsqrt(total, mean, root, tmp, dst, nth):
                link(nc.vector.tensor_scalar(mean, total, 1.0 / D, EPS, ALU.mult, ALU.add))
                nc.vector.reciprocal(root, mean).then_inc(sqrt_in, 1)
                dve.wait_ge(sqrt_out, nth)
                link(nc.vector.tensor_tensor(tmp, root, root, ALU.mult))
                link(nc.vector.tensor_tensor(tmp, tmp, mean, ALU.mult))
                link(nc.vector.tensor_scalar(tmp, tmp, -0.5, 1.5, ALU.mult, ALU.add))
                return nc.vector.tensor_tensor(dst, root, tmp, ALU.mult)

            dve.wait_ge(rows_turned, 1)
            nc.vector.tensor_copy(cT[:, :], ps[0][:, 0:NC]).then_inc(table_ready, 1)
            for j in range(RING):
                lo(1, j, j, j)
            for k in range(KD):
                dve.wait_ge(x_hi_ready, k + 1)
                nc.vector.tensor_tensor(x_lo[:, k, :], ps[4 + k % 4][:, :], f(x_hi[:, k, :]),
                                        ALU.subtract).then_inc(x_lo_ready, 1)
            dve.wait_ge(table_ready, 1)
            lm = cT[:, C_LAM:C_LAM + KR]
            absl, e, s, s2, po, mx = (lam[:, n, :] for n in range(6))
            link(nc.vector.tensor_scalar(mx, lm, -1.0, 0.0, ALU.mult, ALU.max))
            nc.vector.scalar_tensor_tensor(absl, mx, 2.0, lm, ALU.mult, ALU.add).then_inc(lam_exp, 1)
            dve.wait_ge(lam_exp, 2)
            link(nc.vector.tensor_scalar(s, e, 2.0, None, ALU.add))
            link(nc.vector.reciprocal(s, s))
            link(nc.vector.tensor_tensor(s, s, e, ALU.mult))
            link(nc.vector.tensor_tensor(s2, s, s, ALU.mult))
            link(nc.vector.tensor_scalar(po, s2, 1 / 19, None, ALU.mult))
            for term in LOG1P_TERMS:
                link(nc.vector.scalar_tensor_tensor(po, po, term, s2, ALU.add, ALU.mult))
            link(nc.vector.scalar_tensor_tensor(po, po, 1.0, s, ALU.add, ALU.mult))
            link(nc.vector.scalar_tensor_tensor(po, po, 2.0, mx, ALU.mult, ALU.add))
            nc.vector.tensor_scalar(c_pos[:, :], po, LRU_C, None, ALU.mult)
            link(nc.vector.tensor_scalar(c_neg[:, :], po, -LRU_C, None, ALU.mult))
            dve.wait_ge(ss_ready, TT)
            rsqrt(ss[:, :], small[:, 0, :], small[:, 1, :], small[:, 2, :], rs_tok[:, :], 1).then_inc(rs_stored, 1)
            for j in range(RING, AHEAD):
                lo(1, j, j % RING, j)

            def work1(it, pos):
                for b in range(2):
                    rel = pos - 18 * b
                    t0 = it * 4 + 2 * b
                    if rel == 8:
                        dve.wait_ge(w_used, it * N1 + (U1 + 18 * b + 8))
                        for m in range(2):
                            nc.vector.tensor_tensor(ib[:, m, :], ps[m][:, :], rb[:, :],
                                                    ALU.mult).then_inc(xb_taken, 1)
                    if rel in (9, 10):
                        for tap in (0, 1) if rel == 9 else (2, 3):
                            for m in range(2):
                                wc = cT[:, bass.ds(t0 + (C_CONV + KR * tap + m), 1)]
                                src = xbp[:, m, tap:tap + S]
                                if tap == 0:
                                    dve.wait_ge(xb_taken, t0 + (m + 1))
                                    ins = nc.vector.tensor_scalar(xc[:, m, :], src, wc,
                                                                  cT[:, bass.ds(t0 + (C_CB + m), 1)],
                                                                  ALU.mult, ALU.add)
                                else:
                                    dve.wait_ge(conv_step, it * 16 + (8 * b + 2 * tap - 1 + m))
                                    ins = nc.vector.scalar_tensor_tensor(xc[:, m, :], src, wc, xc[:, m, :],
                                                                         ALU.mult, ALU.add)
                                ins.then_inc(conv_step, 1)
                    if rel == 16:
                        dve.wait_ge(y_lo_ready, t0 + 1)
                        for m in range(2):
                            nc.vector.tensor_tensor(gate[:, m, :], ps[2 + m][:, :], rb[:, :],
                                                    ALU.mult).then_inc(gate_taken, 1)
                    if rel == 17:
                        for m in range(2):
                            dve.wait_ge(gate_sig, t0 + (m + 1))
                            nc.vector.tensor_tensor(gate[:, m, :], gate[:, m, :], rbuf[:, m, :],
                                                    ALU.mult).then_inc(gate_ready, 1)
                    if rel == 20:
                        for m in range(2):
                            dve.wait_ge(a2_ready, t0 + (m + 1))
                            nc.vector.scalar_tensor_tensor(tbuf[:, m, :], rbuf[:, m, :], 1.0, tbuf[:, m, :],
                                                           ALU.add, ALU.mult).then_inc(expm1_ready, 1)
                        for m in range(2):
                            dve.wait_ge(expm1_ready, t0 + (m + 1))
                            nc.vector.tensor_scalar(tbuf[:, m, :], tbuf[:, m, :], 0.0, None,
                                                    ALU.max).then_inc(v_ready, 1)
                    if rel == 22:
                        for m in range(2):
                            dve.wait_ge(m_ready, t0 + (m + 1))
                            dve.wait_ge(ix_ready, t0 + (m + 1))
                            nc.vector.tensor_tensor(tbuf[:, m, :], tbuf[:, m, :], ib[:, m, :],
                                                    ALU.mult).then_inc(u_ready, 1)
                        for m in range(2):
                            dve.wait_ge(u_ready, t0 + (m + 1))
                            nc.vector.tensor_tensor_scan(rbuf[:, m, :], abuf[:, m, :], tbuf[:, m, :], 0.0,
                                                         ALU.mult, ALU.add).then_inc(h_ready, 1)
                    if rel == 23:
                        for m in range(2):
                            dve.wait_ge(h_ready, t0 + (m + 1))
                            nc.vector.tensor_tensor(gate[:, m, :], rbuf[:, m, :], gate[:, m, :],
                                                    ALU.mult).then_inc(y_ready, 1)

            def body1(it, last):
                for q in range(N1):
                    lo_at(1, N1, U1, it, last, q)
                    work1(it, q + LOOK)

            dve.wait_ge(rb_in, 16)
            dve.wait_ge(y_lo_ready, 1)
            with dve.Fori(0, B1 - 1) as it:
                body1(it, False)
            body1(B1 - 1, True)

            def work2(it, pos):
                for b in range(2):
                    if pos == 10 * b + 10:
                        dve.wait_ge(w_used, it * N2 + (U2 + 10 * b + 10))
                        for part in range(2):
                            for m in range(2):
                                tile = bass.ds(it * 4 + (2 * b + m), 1)
                                if part == 0:
                                    ins = nc.vector.tensor_tensor(x1[:, m:m + 1, :],
                                                                  ps[2 * b + m][:, :].rearrange("p (a n) -> p a n", a=1),
                                                                  f(x_hi[:, tile, :]), ALU.add)
                                else:
                                    dve.wait_ge(res_step, it * 8 + (4 * b + m + 1))
                                    ins = nc.vector.tensor_tensor(x1[:, m:m + 1, :], x1[:, m:m + 1, :],
                                                                  f(x_lo[:, tile, :]), ALU.add)
                                ins.then_inc(res_step, 1)
                    if pos == 10 * b + 12:
                        for m in range(2):
                            tile = bass.ds(it * 4 + (2 * b + m), 1)
                            dve.wait_ge(x1_hi_ready, it * 4 + (2 * b + m + 1))
                            nc.vector.tensor_tensor(x_lo[:, tile, :], x1[:, m:m + 1, :], f(x_hi[:, tile, :]),
                                                    ALU.subtract).then_inc(x1_lo_ready, 1)

            def body2(it, last):
                for q in range(N2):
                    lo_at(2, N2, U2, it, last, q)
                    work2(it, q + LOOK)
                    if last and q + LOOK == 26:
                        dve.wait_ge(stat_ready, 2)
                        link(rsqrt(ps[4][:, :], nrm[:, 0, :], nrm[:, 1, :], nrm[:, 2, :], rb[:, :], 2))
                        link(nc.vector.tensor_copy(ss[:, :], ps[5][:, 0:TT]))
                        rsqrt(ss[:, :], small[:, 0, :], small[:, 1, :], small[:, 2, :], rs_tok[:, :], 3)\
                            .then_inc(norm2_ready, 1)

            with dve.Fori(0, B2 - 1) as it:
                body2(it, False)
            body2(B2 - 1, True)
            dve.wait_ge(norm2_ready, 1)

            def sticks(p, h, tiles):
                for i in tiles:
                    n, idx = P * (i + 1), I_ORDER.index(i)
                    a, w = K_OFF[i], W_OFF[i]
                    dve.wait_ge(sig_ready, p * 16 + (8 * h + 2 * idx + 2))
                    back = keep[:, a + n - 1::-1] if a == 0 else keep[:, a + n - 1:a - 1:-1]
                    nc.vector.tensor_tensor_scan(back, back, back, 1.0, ALU.mult, ALU.bypass).then_inc(stick_ready, 1)
                for i in tiles:
                    n, idx = P * (i + 1), I_ORDER.index(i)
                    a, w = K_OFF[i], W_OFF[i]
                    dve.wait_ge(stick_ready, p * 8 + (4 * h + idx + 1))
                    nc.vector.tensor_tensor(wgt[:, w:w + n], wgt[:, w:w + n], keep[:, a + 1:a + 1 + n],
                                            ALU.mult).then_inc(wgt_ready, 1)

            def turned_lo(p, h):
                for n, (bank, a, w) in enumerate(BANK_COLS):
                    dve.wait_ge(wt_hi_ready, p * 6 + (3 * h + n + 1))
                    nc.vector.tensor_tensor(wt_lo[:, a:a + w], ps[bank][:, 0:w], f(wt_hi[:, a:a + w]),
                                            ALU.subtract).then_inc(wt_lo_ready, 1)

            def out_f(p, h):
                dve.wait_ge(pv_done, p * 2 + (h + 1))
                dve.wait_ge(qk_lo_ready, p * 4 + 4)
                nc.vector.tensor_tensor(kf[:, h, :], ps[7][:, :], sg[:, h, :], ALU.mult).then_inc(o_f, 1)

            def work3(p, pos):
                if pos == 8:
                    dve.wait_ge(w_used, p * N3 + (U3 + 8))
                    for m in range(2):
                        nc.vector.tensor_tensor(sg[:, m, :], ps[m][:, :], rb[:, :], ALU.mult).then_inc(g_taken, 1)
                if pos == 9:
                    for m in range(2):
                        dve.wait_ge(g_sig, p * 2 + (m + 1))
                        nc.vector.tensor_tensor(sg[:, m, :], sg[:, m, :], kf[:, m, :],
                                                ALU.mult).then_inc(sg_ready, 1)
                for at, bank, c in ((16, 2, 0), (24, 0, 2)):
                    if pos == at:
                        dve.wait_ge(w_used, p * N3 + (U3 + at))
                        if c == 0:
                            dve.wait_ge(sg_ready, p * 2 + 2)
                        else:
                            dve.wait_ge(qk_lo_ready, p * 4 + 2)
                        for m in range(2):
                            nc.vector.tensor_tensor(kf[:, m, :], ps[bank + m][:, :], rb[:, :],
                                                    ALU.mult).then_inc(qk_f, 1)
                if pos == 31:
                    for t in range(TT):
                        dve.wait_ge(v_hi_ready, p * 4 + (2 * (t // 2) + 2))
                        nc.vector.scalar_tensor_tensor(v_lo[:, t, :], ps[2 + t // 2][:, 256 * (t % 2):256 * (t % 2) + 256],
                                                       rs_tok[:, t:t + 1], f(v_hi[:, t, :]),
                                                       ALU.mult, ALU.subtract).then_inc(v_lo_ready, 1)
                if pos in (27, 33):
                    sticks(p, pos // 33, (3, 2))
                if pos in (28, 34):
                    sticks(p, pos // 34, (0, 1))
                if pos in (30, 36):
                    turned_lo(p, pos // 36)
                if pos in (34, 38):
                    out_f(p, pos // 38)

            def body3(p, last):
                for q in range(N3):
                    lo_at(3, N3, U3, p, last, q)
                    work3(p, q + LOOK)

            with dve.Fori(0, B3 - 1) as it:
                body3(it, False)
            body3(B3 - 1, True)

            dve.wait_ge(g_fin_in, 16)

            def take(c):
                for t in range(TT):
                    dve.wait_ge(x2_sq, TT * c + t + 1)
                    nc.vector.tensor_tensor(x2[:, t, 512 * c:512 * c + 512], ps[4 * (c % 2) + t][:, :],
                                            g_fin[:, 512 * c:512 * c + 512], ALU.mult).then_inc(x2_taken, 1)

            for u in range(AHEAD, N4):
                lo(4, u, u % RING, U4 + u)
                if u - RING in (17, 33, 49):
                    take((u - RING) // 16 - 1)
            take(3)
            link(nc.vector.tensor_reduce(ss[:, :], ss4[:, :, :], AX.X, ALU.add))
            rsqrt(ss[:, :], small[:, 0, :], small[:, 1, :], small[:, 2, :], rs_tok[:, :], 4).then_inc(small_step, 1)
            dve.wait_ge(small_step, 1)
            dve.wait_ge(x2_taken, 4 * TT)
            for t in (1, 3):
                nc.vector.tensor_scalar(x2[:, t, :], x2[:, t, :], rs_tok[:, t:t + 1], None,
                                        ALU.mult).then_inc(scaled[t], 1)

        @block.gpsimd
        def _(pool):
            nc.gpsimd.memset(ident[:, :], 0.0).then_inc(id_made, 1)
            nc.gpsimd.memset(ones[:, :], 1.0).then_inc(id_made, 1)
            nc.gpsimd.memset(mask_f[:, :], 0.0).then_inc(id_made, 1)
            pool.wait_ge(id_made, 3)
            nc.gpsimd.affine_select(out=ident[:, :], in_=ident[:, :], compare_op=ALU.not_equal, fill=1.0, base=0,
                                    pattern=[[-1, P]], channel_multiplier=1).then_inc(id_made, 1)
            nc.gpsimd.affine_select(out=mask_f[:, :], in_=mask_f[:, :], compare_op=ALU.is_gt, fill=MASKED,
                                    base=0, pattern=[[-1, P]], channel_multiplier=1).then_inc(id_made, 1)
            pool.wait_ge(id_made, 5)
            nc.gpsimd.tensor_copy(ident_r[:, :], ident[:, :]).then_inc(id_made, 1)
            nc.gpsimd.tensor_copy(mask_r[:, :], mask_f[:, :]).then_inc(id_made, 1)
            pool.wait_ge(ss_ready, TT)
            pool.wait_ge(x_turned, KD)
            nc.gpsimd.memset(xbp[:, :, 0:3], 0.0).then_inc(y_lo_ready, 1)

            with pool.Fori(0, BLOCKS) as n:
                for m in range(2):
                    pool.wait_ge(xc_hi_ready, n * 2 + (m + 1))
                    nc.gpsimd.tensor_tensor(xc_lo[:, m, :], xc[:, m, :], f(xc_hi[:, m, :]),
                                            ALU.subtract).then_inc(xc_lo_ready, 1)
                for m in range(2):
                    pool.wait_ge(ri_ready, n * 4 + (m + 3))
                    nc.gpsimd.tensor_tensor(ib[:, m, :], ib[:, m, :], xc[:, m, :], ALU.mult).then_inc(ix_ready, 1)
                for m in range(2):
                    pool.wait_ge(y_hi_ready, n * 2 + (m + 1))
                    nc.gpsimd.tensor_tensor(y_lo[:, bass.ds(n * 2 + m, 1), :], gate[:, m:m + 1, :],
                                            f(y_hi[:, bass.ds(n * 2 + m, 1), :]),
                                            ALU.subtract).then_inc(y_lo_ready, 1)

            for half in range(2):
                nc.gpsimd.memset(acc[:, 256 * half:256 * half + 256], 0.0).then_inc(acc_step, 1)
            with pool.Fori(0, KD // 2) as n:
                for m in range(2):
                    pool.wait_ge(sq_ready, n * 2 + (m + 1))
                    pool.wait_ge(acc_step, n * 2 + (m + 2))
                    nc.gpsimd.tensor_tensor(acc[:, :], acc[:, :], sq[:, m, :], ALU.add).then_inc(acc_step, 1)

            pool.wait_ge(norm2_ready, 1)
            nc.gpsimd.memset(keep[:, :], 1.0).then_inc(o_lo_ready, 1)
            with pool.Fori(0, PAIRS) as p:
                for dst, src, c in ((q_lo, q_hi, 0), (k_lo, k_hi, 2)):
                    for m in range(2):
                        pool.wait_ge(qk_hi_ready, p * 4 + (c + m + 1))
                        nc.gpsimd.tensor_tensor(dst[:, m, :], kf[:, m, :], f(src[:, m, :]),
                                                ALU.subtract).then_inc(qk_lo_ready, 1)
                for h in range(2):
                    pool.wait_ge(o_hi_ready, p * 2 + (h + 1))
                    nc.gpsimd.tensor_tensor(o_lo[:, bass.ds(p * 2 + h, 1), :], kf[:, h:h + 1, :],
                                            f(o_hi[:, bass.ds(p * 2 + h, 1), :]),
                                            ALU.subtract).then_inc(o_lo_ready, 1)


_INS = ["x", "a_norm", "a_w_in", "a_conv_w", "a_conv_b", "a_w_r", "a_b_r", "a_w_i", "a_b_i", "a_lambda",
        "a_w_out", "kv_norm", "w_kv", "b_norm", "b_w_in", "b_w_out", "final_norm"]


def kernel(**inputs):
    import numpy as _np
    import concourse.bacc as _bacc
    from concourse import mybir as _mybir
    from concourse.bass_utils import run_bass_kernel_spmd as _run

    nc = _bacc.Bacc("TRN2", target_bir_lowering=False, num_devices=1, dynamic_dma_scratch_size=1024)
    f32 = _mybir.dt.float32
    arrays, args = {}, []
    for name in _INS:
        a = _np.ascontiguousarray(inputs[name])
        arrays[f"in_{name}"] = a
        args.append(nc.dram_tensor(f"in_{name}", a.shape, _mybir.dt.from_np(a.dtype), kind="ExternalInput").ap())
    args.append(nc.dram_tensor("out_0", (1, S, D), f32, kind="ExternalOutput").ap())
    args.append(nc.dram_tensor("rs_scratch", (TT, P), f32, kind="Internal").ap())
    build(nc, *args)
    r = _run(nc, [arrays], core_ids=[0])
    return r.results[0]["out_0"]
```

```python
from contextlib import ExitStack

import concourse.bass as bass
from concourse import mybir

F32 = mybir.dt.float32
F32R = mybir.dt.float32r
ACT = mybir.ActivationFunctionType
ALU = mybir.AluOpType
AX = mybir.AxisListType

P = 128
S = 512
D = 2048
R = 2560
KD = D // P
KR = R // P
TT = S // P
HEADS = 16
PAIRS = HEADS // 2
BLOCKS = 10
EPS = 1e-6
LRU_C = 8.0
SCALE = float(P) ** -0.5

RING = 4
AHEAD = 12
LOOK = AHEAD - RING
TURN = 10
N1, N2, N3, N4 = 36, 20, 32, 64
B1, B2, B3 = BLOCKS // 2, KD // 4, PAIRS
U1 = 0
U2 = U1 + N1 * B1
U3 = U2 + N2 * B2
U4 = U3 + N3 * B3
UEND = U4 + N4

C_CONV, C_CB, C_BR, C_BI, C_LAM, C_GKV, C_GB, C_GA = 0, 80, 100, 120, 140, 160, 176, 192
NC = 208
GAIN_ROWS, A_ROWS, B_ROWS = (C_GA, KD), (0, C_BI), (C_BI, C_GA - C_BI)
X_CHUNKS = (0, 2, 4, 8, 12, 16)
FULL_GROUPS, U_HALF, U_LAST = 3, 48, 56

Z_AT = {3: (4, 0), 2: (5, 0), 0: (5, 384), 1: (6, 0)}
WT_AT = {0: (4, 0), 1: (5, 0), 3: (5, 384), 2: (6, 0)}
W_OFF = {0: 0, 1: 128, 2: 384, 3: 768}
K_OFF = {0: 0, 1: 129, 2: 386, 3: 771}
WT_OFF = {0: 0, 1: 512, 3: 896, 2: 1024}
BANK_COLS = ((4, 0, 512), (5, 512, 512), (6, 1024, 256))
I_ORDER = (3, 2, 0, 1)
LOG1P_TERMS = (1 / 17, 1 / 15, 1 / 13, 1 / 11, 1 / 9, 1 / 7, 1 / 5, 1 / 3)


def build(nc, x, a_norm, a_w_in, a_conv_w, a_conv_b, a_w_r, a_b_r, a_w_i, a_b_i, a_lambda, a_w_out,
          kv_norm, w_kv, b_norm, b_w_in, b_w_out, final_norm, out):
    with ExitStack() as ctx:
        def sb(name, shape, dt=F32, scope=ctx):
            return scope.enter_context(nc.sbuf_tensor(name, shape, dt))

        def sem(name):
            return ctx.enter_context(nc.semaphore(name))

        stage = sb("stage", [P, RING, 512])
        w_hi = sb("w_hi", [P, RING, 512], F32R)
        w_lo = sb("w_lo", [P, RING, 512], F32R)
        x_hi = sb("x_hi", [P, KD, S], F32R)
        x_lo = sb("x_lo", [P, KD, S], F32R)
        rb = sb("rb", [P, S])
        ident = sb("ident", [P, P])
        ones = sb("ones", [P, P])
        cT = sb("cT", [P, NC])
        lam = sb("lam", [P, 6, KR])
        c_pos = sb("c_pos", [P, KR])
        c_neg = sb("c_neg", [P, KR])
        ss = sb("ss", [P, TT])
        diag = sb("diag", [P, TT, P])
        rs_tok = sb("rs_tok", [P, TT])
        small = sb("small", [P, 3, TT])
        ss5 = sb("ss5", [P, TT, 5])

        with ExitStack() as mem12:
            y_hi = sb("y_hi", [P, KR, S], F32R, mem12)
            y_lo = sb("y_lo", [P, KR, S], F32R, mem12)
            with ExitStack() as mem0:
                xraw = sb("xraw", [P, TT, D], F32, mem0)
                rows_a = sb("rows_a", [P, P], F32, mem0)
                rows_b = sb("rows_b", [P, P], F32, mem0)
                rows_g = sb("rows_g", [P, P], F32, mem0)
            with ExitStack() as mem1:
                xbp = sb("xbp", [P, 2, S + 4], F32, mem1)
                xc = sb("xc", [P, 2, S], F32, mem1)
                xc_hi = sb("xc_hi", [P, 2, S], F32R, mem1)
                xc_lo = sb("xc_lo", [P, 2, S], F32R, mem1)
                gate = sb("gate", [P, 2, S], F32, mem1)
                rbuf = sb("rbuf", [P, 2, S], F32, mem1)
                tbuf = sb("tbuf", [P, 2, S], F32, mem1)
                abuf = sb("abuf", [P, 2, S], F32, mem1)
            with ExitStack() as mem2:
                x1 = sb("x1", [P, 2, S], F32, mem2)
                sq = sb("sq", [P, 2, S], F32, mem2)
                acc = sb("acc", [P, S], F32, mem2)
        with ExitStack() as mem34:
            o_hi = sb("o_hi", [P, HEADS, S], F32R, mem34)
            o_lo = sb("o_lo", [P, HEADS, S], F32R, mem34)
            x1_f = sb("x1_f", [P, 4, S], F32, mem34)
            with ExitStack() as mem3:
                masked = sb("masked", [P, S], F32, mem3)
                seen = sb("seen", [P, P], F32, mem3)
                q_hi = sb("q_hi", [P, 2, S], F32R, mem3)
                q_lo = sb("q_lo", [P, 2, S], F32R, mem3)
                k_hi = sb("k_hi", [P, 2, S], F32R, mem3)
                k_lo = sb("k_lo", [P, 2, S], F32R, mem3)
                v_hi = sb("v_hi", [P, TT, 2 * P], F32R, mem3)
                v_lo = sb("v_lo", [P, TT, 2 * P], F32R, mem3)
                sg = sb("sg", [P, 2, S], F32, mem3)
                kf = sb("kf", [P, 2, S], F32, mem3)
                keep = sb("keep", [P, 1284], F32, mem3)
                wgt = sb("wgt", [P, 1280], F32, mem3)
                wt_hi = sb("wt_hi", [P, 1280], F32R, mem3)
                wt_lo = sb("wt_lo", [P, 1280], F32R, mem3)
            with ExitStack() as mem4:
                x2 = sb("x2", [P, TT, D], F32, mem4)
                g_fin = sb("g_fin", [P, D], F32, mem4)
                last_hi = sb("last_hi", [P, 4, 512], F32R, mem4)
                last_lo = sb("last_lo", [P, 4, 512], F32R, mem4)
        ib = xbp[:, :, 3:3 + S]

        ps = [ctx.enter_context(nc.psum_tensor(f"ps{b}", [P, S], F32)) for b in range(8)]

        x_in = [sem(f"x_in{c}") for c in range(len(X_CHUNKS) - 1)]
        gain_in = sem("gain_in")
        rows_in = sem("rows_in")
        g_fin_in = sem("g_fin_in")
        stage_full = [sem(f"stage_full{s}") for s in range(RING)]
        hi_ready = sem("hi_ready")
        lo_ready = sem("lo_ready")
        w_used = sem("w_used")
        id_made = sem("id_made")
        mask_made = sem("mask_made")
        rows_turned = sem("rows_turned")
        table_ready = sem("table_ready")
        x_turned = sem("x_turned")
        x_hi_ready = sem("x_hi_ready")
        x_lo_ready = sem("x_lo_ready")
        lam_exp = sem("lam_exp")
        dve_small = sem("dve_small")
        ss_ready = sem("ss_ready")
        sqrt_in = sem("sqrt_in")
        sqrt_out = sem("sqrt_out")
        diag_ready = sem("diag_ready")
        rs_spread = sem("rs_spread")
        rb_ready = sem("rb_ready")
        xb_taken = sem("xb_taken")
        conv_step = sem("conv_step")
        xc_hi_ready = sem("xc_hi_ready")
        xc_lo_ready = sem("xc_lo_ready")
        gate_taken = sem("gate_taken")
        gate_sig = sem("gate_sig")
        gate_ready = sem("gate_ready")
        ri_ready = sem("ri_ready")
        a_ready = sem("a_ready")
        a2_ready = sem("a2_ready")
        expm1_ready = sem("expm1_ready")
        ix_ready = sem("ix_ready")
        v_ready = sem("v_ready")
        m_ready = sem("m_ready")
        u_ready = sem("u_ready")
        h_ready = sem("h_ready")
        y_ready = sem("y_ready")
        y_hi_ready = sem("y_hi_ready")
        y_lo_ready = sem("y_lo_ready")
        res_step = sem("res_step")
        sq_ready = sem("sq_ready")
        x1_hi_ready = sem("x1_hi_ready")
        x1_lo_ready = sem("x1_lo_ready")
        acc_step = sem("acc_step")
        stat_ready = sem("stat_ready")
        g_taken = sem("g_taken")
        g_sig = sem("g_sig")
        sg_ready = sem("sg_ready")
        qk_f = sem("qk_f")
        qk_hi_ready = sem("qk_hi_ready")
        qk_lo_ready = sem("qk_lo_ready")
        v_hi_ready = sem("v_hi_ready")
        v_lo_ready = sem("v_lo_ready")
        z_ready = sem("z_ready")
        sig_ready = sem("sig_ready")
        stick_ready = sem("stick_ready")
        wgt_masked = sem("wgt_masked")
        wgt_ready = sem("wgt_ready")
        wt_turned = sem("wt_turned")
        wt_hi_ready = sem("wt_hi_ready")
        wt_lo_ready = sem("wt_lo_ready")
        pv_done = sem("pv_done")
        o_f = sem("o_f")
        o_hi_ready = sem("o_hi_ready")
        o_lo_ready = sem("o_lo_ready")
        x1_f_ready = sem("x1_f_ready")
        x1_f_used = sem("x1_f_used")
        tile_done = sem("tile_done")
        x2_taken = sem("x2_taken")
        x2_sq = sem("x2_sq")
        rs_ready = sem("rs_ready")
        scaled_a = sem("scaled_a")
        scaled_b = sem("scaled_b")
        stored = sem("stored")

        def f(ap):
            return ap.bitcast(F32)

        def gain_column(phase, j):
            if phase == 1:
                return C_GA + 2 * (j % 18 % 8) if j % 18 < 16 else None
            if phase == 3:
                return (C_GB if j // 8 < 2 else C_GKV) + 2 * (j % 8)
            return None

        def ahead(phase, n, last, q):
            u = q + AHEAD
            if u < n or not last:
                return phase, u % n, u
            return phase + 1, u - n, u

        block = ctx.enter_context(nc.Block())

        @block.sync
        def _(sp):
            def load(src, j, first, u):
                if not first:
                    sp.wait_ge(lo_ready, u - RING + 1)
                dst = stage[:, j % RING, :]
                if src.shape[0] == 2 * P:
                    dst = dst.rearrange("p (k c) -> p k c", k=2)
                    src = src.rearrange("(k p) c -> p k c", p=P)
                sp.dma_start(dst, src).then_inc(stage_full[j % RING], 16)

            def at(col, width=256):
                return bass.ds(col if isinstance(col, int) else sp.snap(col), width)

            def src1(n, j):
                j = j % 18
                if j >= 16:
                    w = a_w_r if j == 16 else a_w_i
                    return w[0, at(n, 1), :, :].rearrange("a r c -> (a r) c")
                return a_w_in[0, 256 * (j % 8):256 * (j % 8) + 256, at(n * 256 + (j // 8) * R)]

            def src3(p, j):
                w, half = ((b_w_in[0], 1), (b_w_in[0], 0), (w_kv, 0), (w_kv, 1))[j // 8]
                w = w.rearrange("r (n c) -> n r c", c=256)
                return w[at(p + half * PAIRS, 1), 256 * (j % 8):256 * (j % 8) + 256, :].rearrange("n r c -> (n r) c")

            def rows_of(dst, first, src, signal):
                sp.dma_start(dst[first:first + src.shape[0], :], src).then_inc(signal, 16)

            def load_x(c):
                a, b = P * X_CHUNKS[c], P * X_CHUNKS[c + 1]
                sp.dma_start(xraw[:, :, a:b], x_v[:, :, a:b]).then_inc(x_in[c], 16)

            def by_tile(v):
                return v.rearrange("a (t p) -> (a t) p", p=P)

            x_v = x.rearrange("b (t p) n -> p (b t) n", p=P)
            rows_of(rows_g, 0, by_tile(a_norm), gain_in)
            load(src1(0, 0), 0, True, 0)
            load_x(0)
            for c in range(1, 4):
                load_x(c)
                load(src1(0, c), c, True, c)
            load_x(4)
            for dst, first, src in ((rows_a, 0, a_conv_w.rearrange("a k (t p) -> (a k t) p", p=P)),
                                    (rows_a, 80, by_tile(a_conv_b)), (rows_a, 100, by_tile(a_b_r)),
                                    (rows_b, 0, by_tile(a_b_i)), (rows_b, 20, by_tile(a_lambda)),
                                    (rows_b, C_GKV - C_BI, kv_norm.rearrange("(t p) -> t p", p=P)),
                                    (rows_b, C_GB - C_BI, by_tile(b_norm))):
                rows_of(dst, first, src, rows_in)
            for j in range(RING, N1):
                load(src1(j // 18, j), j, False, U1 + j)
            with sp.Fori(1, B1) as it:
                for j in range(N1):
                    load(src1(it * 2 + j // 18, j), j, False, it * N1 + (U1 + j))
            with sp.Fori(0, B2) as it:
                for j in range(N2):
                    rows = 256 * (j % 10)
                    load(a_w_out[0, rows:rows + 256, at(it * 512 + 256 * (j // 10))], j, False,
                         it * N2 + (U2 + j))
            with sp.Fori(0, B3) as it:
                for j in range(N3):
                    load(src3(it, j), j, False, it * N3 + (U3 + j))
            for j in range(N4):
                if j < U_HALF:
                    k, c = j % KD, j // KD
                    src = b_w_out[0, P * k:P * k + P, 512 * c:512 * c + 512]
                else:
                    k, c = 2 * (j % 8), 6 + (j - U_HALF) // 8
                    src = b_w_out[0, P * k:P * k + 2 * P, 256 * c:256 * c + 256]
                load(src, j, False, U4 + j)
                if j == 14:
                    sp.wait_ge(o_lo_ready, 1 + HEADS)
                    g_row = final_norm.rearrange("(a n) -> a n", a=1)
                    sp.dma_start(g_fin[:, :], g_row.to_broadcast([P, D])).then_inc(g_fin_in, 16)
            o_v = out.rearrange("b (t p) n -> (b t) p n", p=P)
            for t in range(TT):
                for half, scaled in ((1, scaled_b), (0, scaled_a)):
                    sp.wait_ge(scaled, t + 1)
                    c = D // 2 * half
                    sp.dma_start(o_v[t, :, c:c + D // 2], x2[:, t, c:c + D // 2]).then_inc(stored, 16)
            sp.wait_ge(stored, 16 * 2 * TT)

        @block.tensor
        def _(pe):
            def product(dst, a_hi, a_lo, b_hi, b_lo, start, stop, check=True):
                for n, (a, b) in enumerate(((a_hi, b_hi), (a_hi, b_lo), (a_lo, b_hi))):
                    mm = pe.matmul(dst, a, b, start=start and n == 0, stop=stop and n == 2,
                                   skip_group_check=not check)
                return mm

            def unit_t(j, u, bank, m_hi, m_lo, k0, k_end):
                pe.wait_ge(lo_ready, u + 1)
                s = j % RING
                for kk in range(2):
                    for m in range(2):
                        c = 256 * kk + P * m
                        mm = product(ps[bank + m][:, :], w_hi[:, s, c:c + P], w_lo[:, s, c:c + P],
                                     m_hi[:, k0 + kk, :], m_lo[:, k0 + kk, :],
                                     k0 + kk == 0, k0 + kk == k_end - 1)
                mm.then_inc(w_used, 1)

            def turn_rows(rows, piece):
                c, n = piece
                return pe.transpose(ps[3][:, c:c + n], rows[0:n, :], ident[0:n, 0:n])

            def turn_x(k0):
                if k0 in X_CHUNKS:
                    pe.wait_ge(x_in[X_CHUNKS.index(k0)], 16)
                for k in (k0, k0 + 1):
                    if k >= 4:
                        pe.wait_ge(x_lo_ready, k - 3)
                    for t in range(TT):
                        mm = pe.transpose(ps[4 + k % 4][:, P * t:P * t + P], xraw[:, t, P * k:P * k + P],
                                          ident[:, :])
                    mm.then_inc(x_turned, 1)

            def spread(nth):
                pe.wait_ge(diag_ready, nth)
                pe.matmul(ps[4][:, :], ones[:, :], diag[:, :, :].rearrange("p t n -> p (t n)"),
                          start=True, stop=True).then_inc(rs_spread, 1)

            def unit1(it, j):
                u = it * N1 + (U1 + j)
                b, jj = j // 18, j % 18
                if jj < 16:
                    unit_t(j, u, 2 * (jj // 8), x_hi, x_lo, 2 * (jj % 8), KD)
                else:
                    if jj == 16:
                        pe.wait_ge(xc_lo_ready, it * 4 + (2 * b + 2))
                    unit_t(j, u, 4 + 2 * (jj - 16), xc_hi, xc_lo, 0, 2)

            pe.wait_ge(id_made, 3)
            pe.wait_ge(gain_in, 16)
            turn_rows(rows_g, GAIN_ROWS).then_inc(rows_turned, 1)
            turn_x(0)
            for j in range(8):
                if j < 7:
                    turn_x(2 * j + 2)
                if j == 3:
                    pe.wait_ge(table_ready, 1)
                    pe.wait_ge(rows_in, 16 * 7)
                    turn_rows(rows_a, A_ROWS)
                    turn_rows(rows_b, B_ROWS).then_inc(rows_turned, 1)
                pe.wait_ge(x_lo_ready, 2 * j + 2)
                unit1(0, j)
            for j in range(8, TURN):
                unit1(0, j)
            spread(1)
            with pe.Fori(0, B1 - 1) as it:
                for j in range(TURN, N1 + TURN):
                    unit1(it, j)
            for j in range(TURN, N1):
                unit1(B1 - 1, j)

            with pe.Fori(0, B2) as it:
                for j in range(N2):
                    jj = j % 10
                    if j < 10:
                        pe.wait_ge(y_lo_ready, 1 + 2 * jj + 2)
                    unit_t(j, it * N2 + (U2 + j), 2 * (j // 10), y_hi, y_lo, 2 * jj, KR)

            def proj3(j, u):
                if j < 24:
                    unit_t(j, u, 2 * (j // 8 % 2), x_hi, x_lo, 2 * (j % 8), KD)
                    return
                pe.wait_ge(lo_ready, u + 1)
                s = j % RING
                for kk in range(2):
                    k = 2 * (j % 8) + kk
                    for t in range(TT):
                        mm = product(ps[2 + t // 2][:, 256 * (t % 2):256 * (t % 2) + 256],
                                     x_hi[:, k, P * t:P * t + P], x_lo[:, k, P * t:P * t + P],
                                     w_hi[:, s, 256 * kk:256 * kk + 256], w_lo[:, s, 256 * kk:256 * kk + 256],
                                     k == 0 and t % 2 == 0, k == KD - 1, check=False)
                mm.then_inc(w_used, 1)

            def scores(p, h):
                pe.wait_ge(qk_lo_ready, p * 4 + 4)
                if h == 1:
                    pe.wait_ge(wt_lo_ready, p * 6 + 3)
                for i in I_ORDER:
                    bank, c = Z_AT[i]
                    n = P * (i + 1)
                    mm = product(ps[bank][:, c:c + n], q_hi[:, h, P * i:P * i + P], q_lo[:, h, P * i:P * i + P],
                                 k_hi[:, h, 0:n], k_lo[:, h, 0:n], True, True, check=False)
                    if i != 2:
                        mm.then_inc(z_ready, 1)

            def turn_weights(p, h):
                pe.wait_ge(wgt_ready, p * 8 + (4 * h + 4))
                for k in (0, 1, 3, 2):
                    bank, c = WT_AT[k]
                    for i in range(k, TT):
                        mm = pe.transpose(ps[bank][:, c + P * (i - k):c + P * (i - k) + P],
                                          wgt[:, W_OFF[i] + P * k:W_OFF[i] + P * k + P], ident[:, :])
                    if k != 1:
                        mm.then_inc(wt_turned, 1)

            def values(p, h):
                pe.wait_ge(wt_lo_ready, p * 6 + (3 * h + 3))
                pe.wait_ge(v_lo_ready, p * 4 + 4)
                if h == 1:
                    pe.wait_ge(o_f, p * 2 + 1)
                for k in range(TT):
                    a, n = WT_OFF[k], S - P * k
                    mm = product(ps[7][:, P * k:S], v_hi[:, k, P * h:P * h + P], v_lo[:, k, P * h:P * h + P],
                                 wt_hi[:, a:a + n], wt_lo[:, a:a + n], k == 0, k == TT - 1, check=False)
                mm.then_inc(pv_done, 1)

            for j in range(TURN):
                if j < 8:
                    pe.wait_ge(x1_lo_ready, 2 * j + 2)
                if j == 6:
                    pe.wait_ge(acc_step, 2 + KD)
                    for t in range(TT):
                        mm = pe.matmul(ps[5][:, t:t + 1], acc[:, P * t:P * t + P], ones[:, 0:1],
                                       start=True, stop=True)
                    mm.then_inc(stat_ready, 1)
                proj3(j, U3 + j)
            spread(2)

            def pair_rest(p, next_unit):
                for j in range(TURN, N3 + TURN):
                    if j == 26:
                        scores(p, 0)
                    if j == 30:
                        turn_weights(p, 0)
                    if j == 32:
                        scores(p, 1)
                    if j == 34:
                        values(p, 0)
                    if j == 36:
                        turn_weights(p, 1)
                    if j == 38:
                        values(p, 1)
                    if j < 32:
                        proj3(j, p * N3 + (U3 + j))
                    else:
                        next_unit(j - 32)

            with pe.Fori(0, B3 - 1) as it:
                pair_rest(it, lambda j: proj3(j, it * N3 + (U3 + N3 + j)))

            def add_x1(bank, t, k0, n):
                for m in range(n):
                    mm = pe.matmul(bank[:, P * m:P * m + P], x1_f[:, (k0 + m) % 4, P * t:P * t + P], ident[:, :],
                                   is_transpose=True, start=m == 0, stop=False, skip_group_check=True)
                return mm

            def unit4(j):
                if j < U_HALF:
                    k, c, heads, n = j % KD, j // KD, 1, 4
                else:
                    k, c, heads, n = 2 * (j % 8), FULL_GROUPS, 2, 2
                if c == 0:
                    pe.wait_ge(o_lo_ready, 1 + k + 1)
                if k == 0:
                    pe.wait_ge(x1_f_ready, 4 * c + n)
                pe.wait_ge(lo_ready, U4 + j + 1)
                s, w = j % RING, 512 // heads
                for kk in range(heads):
                    for t in range(TT):
                        if k + kk == 0:
                            if c == 0 and t == 2:
                                pe.wait_ge(v_lo_ready, 4 * PAIRS)
                            turned = add_x1(ps[4 * (c % 2) + t], t, 4 * c, n)
                            if n == 4 and t == TT - 1:
                                turned.then_inc(x1_f_used, 1)
                        mm = product(ps[4 * (c % 2) + t][:, 0:w], o_hi[:, k + kk, P * t:P * t + P],
                                     o_lo[:, k + kk, P * t:P * t + P], w_hi[:, s, w * kk:w * kk + w],
                                     w_lo[:, s, w * kk:w * kk + w], False, k + kk == KD - 1, check=False)
                mm.then_inc(w_used, 1)

            def last_columns():
                pe.wait_ge(x1_f_ready, KD)
                for t in range(TT):
                    add_x1(ps[t], t, KD - 2, 2)
                    for j in range(8):
                        if t == 0:
                            pe.wait_ge(lo_ready, U4 + U_LAST + j + 1)
                        hi_w, lo_w = (last_hi, last_lo) if j < 4 else (w_hi, w_lo)
                        for kk in range(2):
                            k, c = 2 * j + kk, 256 * kk
                            mm = product(ps[t][:, 0:256], o_hi[:, k, P * t:P * t + P], o_lo[:, k, P * t:P * t + P],
                                         hi_w[:, j % 4, c:c + 256], lo_w[:, j % 4, c:c + 256],
                                         False, k == KD - 1, check=False)
                    mm.then_inc(tile_done, 1)

            pair_rest(B3 - 1, unit4)
            for j in range(TURN, U_LAST):
                unit4(j)
            last_columns()

        @block.scalar
        def _(act):
            def split_hi(phase, j, slot):
                col = gain_column(phase, j)
                if col is None:
                    nc.scalar.activation(w_hi[:, slot, :], stage[:, slot, :], ACT.Copy).then_inc(hi_ready, 1)
                    return
                nc.scalar.activation(w_hi[:, slot, 0:256], stage[:, slot, 0:256], ACT.Identity,
                                     scale=cT[:, col:col + 1])
                nc.scalar.activation(w_hi[:, slot, 256:512], stage[:, slot, 256:512], ACT.Identity,
                                     scale=cT[:, col + 1:col + 2]).then_inc(hi_ready, 1)

            def hi(phase, j, u):
                act.wait_ge(stage_full[u % RING], 16 * (u // RING + 1))
                if u >= RING:
                    act.wait_ge(w_used, u - RING + 1)
                split_hi(phase, j, u % RING)

            def hi_at(phase, n, base, it, last, q):
                ph, j, off = ahead(phase, n, last, q)
                slot = off % RING
                first = base + off - slot
                act.wait_ge(stage_full[slot], it * (4 * n) + (4 * first + 16))
                act.wait_ge(w_used, it * n + (base + off - RING + 1))
                split_hi(ph, j, slot)

            def x_parts(a, b):
                for k in range(a, b):
                    act.wait_ge(x_turned, k + 1)
                    nc.scalar.copy(x_hi[:, k, :], ps[4 + k % 4][:, :]).then_inc(x_hi_ready, 1)

            act.wait_ge(table_ready, 1)
            hi(1, 0, U1)
            for j in range(8):
                x_parts(2 * j, 2 * j + 2)
                if j:
                    hi(1, j, U1 + j)
                if j == 7:
                    hi(1, 8, U1 + 8)
                if j == 4:
                    act.wait_ge(lam_exp, 1)
                    nc.scalar.activation(lam[:, 1, :], lam[:, 0, :], ACT.Exp, scale=-1.0).then_inc(lam_exp, 1)
                if j >= 1:
                    c = (j - 1) // 2
                    for t in (0, 1) if j % 2 else (2, 3):
                        xs = xraw[:, t, 512 * c:512 * c + 512]
                        nc.scalar.activation(xs, xs, ACT.Square, accum_out=ss5[:, t, c:c + 1]).then_inc(ss_ready, 1)
            act.wait_ge(sqrt_in, 1)
            nc.scalar.activation(small[:, 1, :], small[:, 1, :], ACT.Sqrt).then_inc(sqrt_out, 1)
            for j in range(9, AHEAD):
                hi(1, j, U1 + j)

            def work1(it, pos):
                b = 1 if pos >= 26 else 0
                rel = pos - 18 * b
                if rel == 11:
                    for m in range(2):
                        act.wait_ge(conv_step, it * 16 + (8 * b + 7 + m))
                        nc.scalar.copy(xc_hi[:, m, :], xc[:, m, :]).then_inc(xc_hi_ready, 1)
                if rel == 16:
                    for m in range(2):
                        act.wait_ge(gate_taken, it * 4 + (2 * b + m + 1))
                        nc.scalar.activation(rbuf[:, m, :], gate[:, m, :], ACT.Sigmoid).then_inc(gate_sig, 1)
                if pos in range(18, 26) or pos in range(36, 44):
                    b = (pos - 18) // 18
                    rel = (pos - 18) % 18
                    t0 = it * 4 + 2 * b
                    if rel == 0:
                        act.wait_ge(w_used, it * N1 + (U1 + 18 * b + 18))
                        for m in range(2):
                            act.wait_ge(gate_ready, it * 4 + (2 * b + m + 1))
                            nc.scalar.activation(rbuf[:, m, :], ps[4 + m][:, :], ACT.Sigmoid,
                                                 bias=cT[:, bass.ds(t0 + (C_BR + m), 1)]).then_inc(ri_ready, 1)
                        for m in range(2):
                            nc.scalar.activation(ib[:, m, :], ps[6 + m][:, :], ACT.Sigmoid,
                                                 bias=cT[:, bass.ds(t0 + (C_BI + m), 1)]).then_inc(ri_ready, 1)
                    if rel == 1:
                        for m in range(2):
                            act.wait_ge(ri_ready, it * 8 + (4 * b + m + 1))
                            nc.scalar.activation(tbuf[:, m, :], rbuf[:, m, :], ACT.Tanh,
                                                 scale=c_pos[:, bass.ds(t0 + m, 1)])
                        for m in range(2):
                            nc.scalar.activation(abuf[:, m, :], rbuf[:, m, :], ACT.Exp,
                                                 scale=c_neg[:, bass.ds(t0 + m, 1)]).then_inc(a_ready, 1)
                        for m in range(2):
                            act.wait_ge(a_ready, it * 4 + (2 * b + m + 1))
                            nc.scalar.activation(rbuf[:, m, :], abuf[:, m, :], ACT.Square).then_inc(a2_ready, 1)
                    if rel == 3:
                        for m in range(2):
                            act.wait_ge(v_ready, it * 4 + (2 * b + m + 1))
                            nc.scalar.activation(tbuf[:, m, :], tbuf[:, m, :], ACT.Sqrt).then_inc(m_ready, 1)
                    if rel == 6:
                        for m in range(2):
                            act.wait_ge(y_ready, it * 4 + (2 * b + m + 1))
                            nc.scalar.copy(y_hi[:, bass.ds(t0 + m, 1), :],
                                           gate[:, m:m + 1, :]).then_inc(y_hi_ready, 1)

            def body1(it, last):
                for q in range(N1):
                    hi_at(1, N1, U1, it, last, q)
                    work1(it, q + LOOK)

            with act.Fori(0, B1 - 1) as it:
                body1(it, False)
            body1(B1 - 1, True)

            def work2(it, pos):
                for b in range(2):
                    if pos == 10 * b + 11:
                        for m in range(2):
                            act.wait_ge(res_step, it * 8 + (4 * b + m + 3))
                            act.wait_ge(acc_step, it * 4 + (2 * b + m + 1))
                            nc.scalar.activation(sq[:, m, :], x1[:, m, :], ACT.Square).then_inc(sq_ready, 1)
                            nc.scalar.copy(x_hi[:, bass.ds(it * 4 + (2 * b + m), 1), :],
                                           x1[:, m:m + 1, :]).then_inc(x1_hi_ready, 1)

            def body2(it, last):
                for q in range(N2):
                    hi_at(2, N2, U2, it, last, q)
                    work2(it, q + LOOK)
                    if last and q + LOOK == 26:
                        act.wait_ge(sqrt_in, 2)
                        nc.scalar.activation(small[:, 1, :], small[:, 1, :], ACT.Sqrt).then_inc(sqrt_out, 1)

            with act.Fori(0, B2 - 1) as it:
                body2(it, False)
            body2(B2 - 1, True)

            def sticks(p, h, tiles):
                for i in tiles:
                    bank, c = Z_AT[i]
                    n = P * (i + 1)
                    act.wait_ge(z_ready, p * 6 + (3 * h + bank - 3))
                    nc.scalar.activation(keep[:, K_OFF[i]:K_OFF[i] + n], ps[bank][:, c:c + n], ACT.Sigmoid,
                                         scale=-SCALE).then_inc(sig_ready, 1)
                    nc.scalar.activation(wgt[:, W_OFF[i]:W_OFF[i] + n], ps[bank][:, c:c + n], ACT.Sigmoid,
                                         scale=SCALE).then_inc(sig_ready, 1)

            def turned_hi(p, h):
                for n, (bank, a, w) in enumerate(BANK_COLS):
                    act.wait_ge(wt_turned, p * 6 + (3 * h + n + 1))
                    nc.scalar.copy(wt_hi[:, a:a + w], ps[bank][:, 0:w]).then_inc(wt_hi_ready, 1)

            def out_hi(p, h):
                act.wait_ge(o_f, p * 2 + (h + 1))
                nc.scalar.copy(o_hi[:, bass.ds(p * 2 + h, 1), :], kf[:, h:h + 1, :]).then_inc(o_hi_ready, 1)

            def work3(p, pos):
                if pos == 8:
                    for m in range(2):
                        act.wait_ge(g_taken, p * 2 + (m + 1))
                        act.wait_ge(o_lo_ready, p * 2 + 1)
                        nc.scalar.activation(kf[:, m, :], sg[:, m, :], ACT.Sigmoid).then_inc(g_sig, 1)
                for at, (dst, c) in ((15, (q_hi, 0)), (23, (k_hi, 2))):
                    if pos == at:
                        for m in range(2):
                            act.wait_ge(qk_f, p * 4 + (c + m + 1))
                            nc.scalar.copy(dst[:, m, :], kf[:, m, :]).then_inc(qk_hi_ready, 1)
                if pos == 31:
                    act.wait_ge(w_used, p * N3 + (U3 + N3))
                    for t in range(TT):
                        nc.scalar.activation(v_hi[:, t, :], ps[2 + t // 2][:, 256 * (t % 2):256 * (t % 2) + 256],
                                             ACT.Identity, scale=rs_tok[:, t:t + 1]).then_inc(v_hi_ready, 1)
                if pos in (25, 31):
                    sticks(p, pos // 31, (3, 2))
                if pos in (26, 32):
                    sticks(p, pos // 32, (0, 1))
                if pos in (29, 35):
                    turned_hi(p, pos // 35)
                if pos in (34, 38):
                    out_hi(p, pos // 38)

            def body3(p, last):
                for q in range(N3):
                    if q + LOOK == 23:
                        work3(p, q + LOOK)
                    hi_at(3, N3, U3, p, last, q)
                    if q + LOOK != 23:
                        work3(p, q + LOOK)

            with act.Fori(0, B3 - 1) as it:
                body3(it, False)
            body3(B3 - 1, True)

            def square(bank, w, t, c, nth):
                act.wait_ge(x2_taken, nth)
                nc.scalar.activation(bank[:, 0:w], bank[:, 0:w], ACT.Square,
                                     accum_out=ss5[:, t, c:c + 1]).then_inc(x2_sq, 1)

            def squares(c):
                for t in range(TT):
                    square(ps[4 * (c % 2) + t], 512 if c < FULL_GROUPS else 256, t, c, TT * c + t + 1)

            for u in range(AHEAD, N4):
                act.wait_ge(stage_full[u % RING], 16 * ((U4 + u) // RING + 1))
                if u < U_LAST:
                    act.wait_ge(w_used, U4 + u - RING + 1)
                    split_hi(4, u, u % RING)
                elif u < U_LAST + 4:
                    nc.scalar.activation(last_hi[:, u % RING, :], stage[:, u % RING, :],
                                         ACT.Copy).then_inc(hi_ready, 1)
                else:
                    act.wait_ge(w_used, U4 + u - 8 + 1)
                    split_hi(4, u, u % RING)
                if u in (20, 36, 52):
                    squares((u - 20) // 16)
            squares(FULL_GROUPS)
            act.wait_ge(lo_ready, UEND)
            for t in range(TT):
                act.wait_ge(tile_done, t + 1)
                nc.scalar.activation(stage[:, 0, 0:256], ps[t][:, 0:256], ACT.Square,
                                     accum_out=ss5[:, t, 4:5]).then_inc(x2_sq, 1)
                act.wait_ge(sqrt_in, 3 + t)
                nc.scalar.activation(small[:, 1, t:t + 1], small[:, 1, t:t + 1], ACT.Sqrt).then_inc(sqrt_out, 1)
                act.wait_ge(rs_ready, 3 + t)
                nc.scalar.activation(x2[:, t, 0:D // 2], x2[:, t, 0:D // 2], ACT.Identity,
                                     scale=rs_tok[:, t:t + 1]).then_inc(scaled_a, 1)

        @block.vector
        def _(dve):
            own = [0]

            def link(ins):
                own[0] += 1
                ins.then_inc(dve_small, 1)
                dve.wait_ge(dve_small, own[0])

            def lo(phase, j, slot, u):
                dve.wait_ge(hi_ready, u + 1)
                col = gain_column(phase, j)
                if col is None:
                    nc.vector.tensor_tensor(w_lo[:, slot, :], stage[:, slot, :], f(w_hi[:, slot, :]),
                                            ALU.subtract).then_inc(lo_ready, 1)
                    return
                nc.vector.scalar_tensor_tensor(w_lo[:, slot, 0:256], stage[:, slot, 0:256], cT[:, col:col + 1],
                                               f(w_hi[:, slot, 0:256]), ALU.mult, ALU.subtract)
                nc.vector.scalar_tensor_tensor(w_lo[:, slot, 256:512], stage[:, slot, 256:512],
                                               cT[:, col + 1:col + 2], f(w_hi[:, slot, 256:512]),
                                               ALU.mult, ALU.subtract).then_inc(lo_ready, 1)

            def lo_at(phase, n, base, it, last, q):
                ph, j, off = ahead(phase, n, last, q)
                lo(ph, j, off % RING, it * n + (base + off))

            def rsqrt(total, mean, root, tmp, dst, nth, meanwhile=None):
                link(nc.vector.tensor_scalar(mean, total, 1.0 / D, EPS, ALU.mult, ALU.add))
                nc.vector.reciprocal(root, mean).then_inc(sqrt_in, 1)
                if meanwhile:
                    meanwhile()
                dve.wait_ge(sqrt_out, nth)
                link(nc.vector.tensor_tensor(tmp, root, root, ALU.mult))
                link(nc.vector.tensor_tensor(tmp, tmp, mean, ALU.mult))
                link(nc.vector.tensor_scalar(tmp, tmp, -0.5, 1.5, ALU.mult, ALU.add))
                nc.vector.tensor_tensor(dst, root, tmp, ALU.mult).then_inc(rs_ready, 1)
                dve.wait_ge(rs_ready, nth)

            def diagonals():
                for t in range(TT):
                    ins = nc.vector.tensor_scalar(diag[:, t, :], ident[:, :], rs_tok[:, t:t + 1], None, ALU.mult)
                ins.then_inc(diag_ready, 1)

            def take_rb(nth):
                dve.wait_ge(rs_spread, nth)
                nc.vector.tensor_copy(rb[:, :], ps[4][:, :]).then_inc(rb_ready, 1)
                dve.wait_ge(rb_ready, nth)

            def x_parts(a, b):
                for k in range(a, b):
                    dve.wait_ge(x_hi_ready, k + 1)
                    nc.vector.tensor_tensor(x_lo[:, k, :], ps[4 + k % 4][:, :], f(x_hi[:, k, :]),
                                            ALU.subtract).then_inc(x_lo_ready, 1)

            def table(piece, nth):
                c, n = piece
                dve.wait_ge(rows_turned, nth)
                return nc.vector.tensor_copy(cT[:, c:c + n], ps[3][:, c:c + n])

            table(GAIN_ROWS, 1).then_inc(table_ready, 1)
            absl, e, s, s2, po, mx = (lam[:, n, :] for n in range(6))
            dve.wait_ge(table_ready, 1)
            lo(1, 0, 0, U1)
            for j in range(8):
                x_parts(2 * j, 2 * j + 2)
                if j:
                    lo(1, j, j % RING, U1 + j)
                if j == 3:
                    table((0, C_GA), 2).then_inc(table_ready, 1)
                    dve.wait_ge(table_ready, 2)
                    lm = cT[:, C_LAM:C_LAM + KR]
                    link(nc.vector.tensor_scalar(mx, lm, -1.0, 0.0, ALU.mult, ALU.max))
                    nc.vector.scalar_tensor_tensor(absl, mx, 2.0, lm, ALU.mult, ALU.add).then_inc(lam_exp, 1)
            lo(1, 8, 8 % RING, U1 + 8)
            dve.wait_ge(x_turned, KD)
            for t in (2, 3):
                xs = xraw[:, t, D - 512:D]
                link(nc.vector.tensor_tensor_reduce(xs, xs, xs, 1.0, 0.0, ALU.mult, ALU.add, ss5[:, t, 3:4]))
            dve.wait_ge(ss_ready, 14)
            link(nc.vector.tensor_reduce(ss[:, :], ss5[:, :, 0:4], AX.X, ALU.add))
            rsqrt(ss[:, :], small[:, 0, :], small[:, 1, :], small[:, 2, :], rs_tok[:, :], 1)
            diagonals()
            for j in range(9, AHEAD):
                lo(1, j, j % RING, U1 + j)
            dve.wait_ge(lam_exp, 2)
            link(nc.vector.tensor_scalar(s, e, 2.0, None, ALU.add))
            link(nc.vector.reciprocal(s, s))
            link(nc.vector.tensor_tensor(s, s, e, ALU.mult))
            link(nc.vector.tensor_tensor(s2, s, s, ALU.mult))
            link(nc.vector.tensor_scalar(po, s2, 1 / 19, None, ALU.mult))
            for term in LOG1P_TERMS:
                link(nc.vector.scalar_tensor_tensor(po, po, term, s2, ALU.add, ALU.mult))
            link(nc.vector.scalar_tensor_tensor(po, po, 1.0, s, ALU.add, ALU.mult))
            link(nc.vector.scalar_tensor_tensor(po, po, 2.0, mx, ALU.mult, ALU.add))
            nc.vector.tensor_scalar(c_pos[:, :], po, LRU_C, None, ALU.mult)
            link(nc.vector.tensor_scalar(c_neg[:, :], po, -LRU_C, None, ALU.mult))
            def work1(it, pos):
                for b in range(2):
                    rel = pos - 18 * b
                    t0 = it * 4 + 2 * b
                    if rel == 8:
                        dve.wait_ge(w_used, it * N1 + (U1 + 18 * b + 8))
                        for m in range(2):
                            nc.vector.tensor_tensor(ib[:, m, :], ps[m][:, :], rb[:, :],
                                                    ALU.mult).then_inc(xb_taken, 1)
                    if rel in (9, 10):
                        for tap in (0, 1) if rel == 9 else (2, 3):
                            for m in range(2):
                                wc = cT[:, bass.ds(t0 + (C_CONV + KR * tap + m), 1)]
                                src = xbp[:, m, tap:tap + S]
                                if tap == 0:
                                    dve.wait_ge(xb_taken, t0 + (m + 1))
                                    ins = nc.vector.tensor_scalar(xc[:, m, :], src, wc,
                                                                  cT[:, bass.ds(t0 + (C_CB + m), 1)],
                                                                  ALU.mult, ALU.add)
                                else:
                                    dve.wait_ge(conv_step, it * 16 + (8 * b + 2 * tap - 1 + m))
                                    ins = nc.vector.scalar_tensor_tensor(xc[:, m, :], src, wc, xc[:, m, :],
                                                                         ALU.mult, ALU.add)
                                ins.then_inc(conv_step, 1)
                    if rel == 16:
                        dve.wait_ge(y_lo_ready, t0 + 1)
                        for m in range(2):
                            nc.vector.tensor_tensor(gate[:, m, :], ps[2 + m][:, :], rb[:, :],
                                                    ALU.mult).then_inc(gate_taken, 1)
                    if rel == 17:
                        for m in range(2):
                            dve.wait_ge(gate_sig, t0 + (m + 1))
                            nc.vector.tensor_tensor(gate[:, m, :], gate[:, m, :], rbuf[:, m, :],
                                                    ALU.mult).then_inc(gate_ready, 1)
                    if rel == 20:
                        for m in range(2):
                            dve.wait_ge(a2_ready, t0 + (m + 1))
                            nc.vector.scalar_tensor_tensor(tbuf[:, m, :], rbuf[:, m, :], 1.0, tbuf[:, m, :],
                                                           ALU.add, ALU.mult).then_inc(expm1_ready, 1)
                        for m in range(2):
                            dve.wait_ge(expm1_ready, t0 + (m + 1))
                            nc.vector.tensor_scalar(tbuf[:, m, :], tbuf[:, m, :], 0.0, None,
                                                    ALU.max).then_inc(v_ready, 1)
                    if rel == 22:
                        for m in range(2):
                            dve.wait_ge(m_ready, t0 + (m + 1))
                            dve.wait_ge(ix_ready, t0 + (m + 1))
                            nc.vector.tensor_tensor(tbuf[:, m, :], tbuf[:, m, :], ib[:, m, :],
                                                    ALU.mult).then_inc(u_ready, 1)
                        for m in range(2):
                            dve.wait_ge(u_ready, t0 + (m + 1))
                            nc.vector.tensor_tensor_scan(rbuf[:, m, :], abuf[:, m, :], tbuf[:, m, :], 0.0,
                                                         ALU.mult, ALU.add).then_inc(h_ready, 1)
                    if rel == 23:
                        for m in range(2):
                            dve.wait_ge(h_ready, t0 + (m + 1))
                            nc.vector.tensor_tensor(gate[:, m, :], rbuf[:, m, :], gate[:, m, :],
                                                    ALU.mult).then_inc(y_ready, 1)

            def body1(it, last):
                for q in range(N1):
                    lo_at(1, N1, U1, it, last, q)
                    work1(it, q + LOOK)

            take_rb(1)
            dve.wait_ge(y_lo_ready, 1)
            with dve.Fori(0, B1 - 1) as it:
                body1(it, False)
            body1(B1 - 1, True)

            def work2(it, pos):
                for b in range(2):
                    if pos == 10 * b + 10:
                        dve.wait_ge(w_used, it * N2 + (U2 + 10 * b + 10))
                        for part in range(2):
                            for m in range(2):
                                tile = bass.ds(it * 4 + (2 * b + m), 1)
                                if part == 0:
                                    sums = ps[2 * b + m][:, :].rearrange("p (a n) -> p a n", a=1)
                                    ins = nc.vector.tensor_tensor(x1[:, m:m + 1, :], sums,
                                                                  f(x_hi[:, tile, :]), ALU.add)
                                else:
                                    dve.wait_ge(res_step, it * 8 + (4 * b + m + 1))
                                    ins = nc.vector.tensor_tensor(x1[:, m:m + 1, :], x1[:, m:m + 1, :],
                                                                  f(x_lo[:, tile, :]), ALU.add)
                                ins.then_inc(res_step, 1)
                    if pos == 10 * b + 12:
                        for m in range(2):
                            tile = bass.ds(it * 4 + (2 * b + m), 1)
                            dve.wait_ge(x1_hi_ready, it * 4 + (2 * b + m + 1))
                            nc.vector.tensor_tensor(x_lo[:, tile, :], x1[:, m:m + 1, :], f(x_hi[:, tile, :]),
                                                    ALU.subtract).then_inc(x1_lo_ready, 1)

            def body2(it, last):
                for q in range(N2):
                    lo_at(2, N2, U2, it, last, q)
                    work2(it, q + LOOK)
                    if last and q + LOOK == 26:
                        dve.wait_ge(stat_ready, 1)
                        rsqrt(ps[5][:, 0:TT], small[:, 0, :], small[:, 1, :], small[:, 2, :], rs_tok[:, :], 2)
                        diagonals()

            with dve.Fori(0, B2 - 1) as it:
                body2(it, False)
            body2(B2 - 1, True)
            take_rb(2)
            dve.wait_ge(mask_made, 3)

            def sticks(p, h, tiles):
                for i in tiles:
                    n, idx = P * (i + 1), I_ORDER.index(i)
                    a, w = K_OFF[i], W_OFF[i]
                    dve.wait_ge(sig_ready, p * 16 + (8 * h + 2 * idx + 2))
                    back = keep[:, a + n - 1::-1] if a == 0 else keep[:, a + n - 1:a - 1:-1]
                    nc.vector.tensor_tensor_scan(back, back, masked[:, S - 1:S - 1 - n if n < S else None:-1], 1.0,
                                                 ALU.mult, ALU.max).then_inc(stick_ready, 1)
                for i in tiles:
                    n, idx = P * (i + 1), I_ORDER.index(i)
                    a, w = K_OFF[i], W_OFF[i]
                    dve.wait_ge(stick_ready, p * 8 + (4 * h + idx + 1))
                    dve.wait_ge(wgt_masked, p * 8 + (4 * h + idx + 1))
                    nc.vector.tensor_tensor(wgt[:, w:w + n], wgt[:, w:w + n], keep[:, a + 1:a + 1 + n],
                                            ALU.mult).then_inc(wgt_ready, 1)

            def turned_lo(p, h):
                for n, (bank, a, w) in enumerate(BANK_COLS):
                    dve.wait_ge(wt_hi_ready, p * 6 + (3 * h + n + 1))
                    nc.vector.tensor_tensor(wt_lo[:, a:a + w], ps[bank][:, 0:w], f(wt_hi[:, a:a + w]),
                                            ALU.subtract).then_inc(wt_lo_ready, 1)

            def out_f(p, h):
                dve.wait_ge(pv_done, p * 2 + (h + 1))
                dve.wait_ge(qk_lo_ready, p * 4 + 4)
                nc.vector.tensor_tensor(kf[:, h, :], ps[7][:, :], sg[:, h, :], ALU.mult).then_inc(o_f, 1)

            def work3(p, pos):
                if pos == 8:
                    dve.wait_ge(w_used, p * N3 + (U3 + 8))
                    for m in range(2):
                        nc.vector.tensor_tensor(sg[:, m, :], ps[m][:, :], rb[:, :], ALU.mult).then_inc(g_taken, 1)
                if pos == 9:
                    for m in range(2):
                        dve.wait_ge(g_sig, p * 2 + (m + 1))
                        nc.vector.tensor_tensor(sg[:, m, :], sg[:, m, :], kf[:, m, :],
                                                ALU.mult).then_inc(sg_ready, 1)
                for at, bank, c in ((15, 2, 0), (23, 0, 2)):
                    if pos == at:
                        dve.wait_ge(w_used, p * N3 + (U3 + at + 1))
                        if c == 0:
                            dve.wait_ge(sg_ready, p * 2 + 2)
                        else:
                            dve.wait_ge(qk_lo_ready, p * 4 + 2)
                        for m in range(2):
                            nc.vector.tensor_tensor(kf[:, m, :], ps[bank + m][:, :], rb[:, :],
                                                    ALU.mult).then_inc(qk_f, 1)
                if pos == 31:
                    for t in range(TT):
                        dve.wait_ge(v_hi_ready, p * 4 + (2 * (t // 2) + 2))
                        v_sums = ps[2 + t // 2][:, 256 * (t % 2):256 * (t % 2) + 256]
                        nc.vector.scalar_tensor_tensor(v_lo[:, t, :], v_sums, rs_tok[:, t:t + 1], f(v_hi[:, t, :]),
                                                       ALU.mult, ALU.subtract).then_inc(v_lo_ready, 1)
                if pos in (26, 32):
                    sticks(p, pos // 32, (3, 2))
                if pos in (27, 33):
                    sticks(p, pos // 33, (0, 1))
                if pos in (29, 35):
                    turned_lo(p, pos // 35)
                if pos in (34, 38):
                    out_f(p, pos // 38)

            def body3(p, last):
                for q in range(N3):
                    if q + LOOK == 23:
                        work3(p, q + LOOK)
                    lo_at(3, N3, U3, p, last, q)
                    if q + LOOK != 23:
                        work3(p, q + LOOK)

            with dve.Fori(0, B3 - 1) as it:
                body3(it, False)
            body3(B3 - 1, True)

            def take(bank, t, c, w):
                nc.vector.tensor_tensor(x2[:, t, c:c + w], bank[:, 0:w], g_fin[:, c:c + w],
                                        ALU.mult).then_inc(x2_taken, 1)

            for u in range(AHEAD, N4):
                if U_LAST <= u < U_LAST + 4:
                    dve.wait_ge(hi_ready, U4 + u + 1)
                    nc.vector.tensor_tensor(last_lo[:, u % RING, :], stage[:, u % RING, :],
                                            f(last_hi[:, u % RING, :]), ALU.subtract).then_inc(lo_ready, 1)
                else:
                    lo(4, u, u % RING, U4 + u)
                if u in (20, 36, 52):
                    c = (u - 20) // 16
                    if c == 0:
                        dve.wait_ge(g_fin_in, 16)
                    dve.wait_ge(w_used, U4 + KD * (c + 1))
                    for t in range(TT):
                        take(ps[4 * (c % 2) + t], t, 512 * c, 512)
            dve.wait_ge(w_used, U4 + U_LAST)
            for t in range(TT):
                take(ps[4 * (FULL_GROUPS % 2) + t], t, 512 * FULL_GROUPS, 256)
            for t in range(TT):
                dve.wait_ge(x2_sq, 4 * TT + t + 1)
                one = slice(t, t + 1)
                link(nc.vector.tensor_reduce(ss[:, one], ss5[:, t, :], AX.X, ALU.add))
                rsqrt(ss[:, one], small[:, 0, one], small[:, 1, one], small[:, 2, one], rs_tok[:, one], 3 + t,
                      lambda: take(ps[t], t, D - 256, 256))
                dve.wait_ge(x2_taken, 4 * TT + t + 1)
                nc.vector.tensor_scalar(x2[:, t, D // 2:D], x2[:, t, D // 2:D], rs_tok[:, one], None,
                                        ALU.mult).then_inc(scaled_b, 1)

        @block.gpsimd
        def _(pool):
            nc.gpsimd.memset(ident[:, :], 0.0).then_inc(id_made, 1)
            nc.gpsimd.memset(ones[:, :], 1.0).then_inc(id_made, 1)
            pool.wait_ge(id_made, 2)
            nc.gpsimd.affine_select(out=ident[:, :], in_=ident[:, :], compare_op=ALU.not_equal, fill=1.0, base=0,
                                    pattern=[[-1, P]], channel_multiplier=1).then_inc(id_made, 1)
            pool.wait_ge(diag_ready, 1)
            nc.gpsimd.memset(xbp[:, :, 0:3], 0.0).then_inc(y_lo_ready, 1)

            with pool.Fori(0, BLOCKS) as n:
                for m in range(2):
                    pool.wait_ge(xc_hi_ready, n * 2 + (m + 1))
                    nc.gpsimd.tensor_tensor(xc_lo[:, m, :], xc[:, m, :], f(xc_hi[:, m, :]),
                                            ALU.subtract).then_inc(xc_lo_ready, 1)
                for m in range(2):
                    pool.wait_ge(ri_ready, n * 4 + (m + 3))
                    nc.gpsimd.tensor_tensor(ib[:, m, :], ib[:, m, :], xc[:, m, :], ALU.mult).then_inc(ix_ready, 1)
                for m in range(2):
                    pool.wait_ge(y_hi_ready, n * 2 + (m + 1))
                    nc.gpsimd.tensor_tensor(y_lo[:, bass.ds(n * 2 + m, 1), :], gate[:, m:m + 1, :],
                                            f(y_hi[:, bass.ds(n * 2 + m, 1), :]),
                                            ALU.subtract).then_inc(y_lo_ready, 1)

            for half in range(2):
                nc.gpsimd.memset(acc[:, 256 * half:256 * half + 256], 0.0).then_inc(acc_step, 1)
            with pool.Fori(0, KD // 2) as n:
                for m in range(2):
                    pool.wait_ge(sq_ready, n * 2 + (m + 1))
                    pool.wait_ge(acc_step, n * 2 + (m + 2))
                    nc.gpsimd.tensor_tensor(acc[:, :], acc[:, :], sq[:, m, :], ALU.add).then_inc(acc_step, 1)

            def below_diagonal(block, fill):
                return nc.gpsimd.affine_select(out=block, in_=block, compare_op=ALU.is_gt, fill=fill, base=0,
                                               pattern=[[-1, P]], channel_multiplier=1)

            def x1_parts(c):
                if c:
                    pool.wait_ge(x1_f_used, c)
                for n in range(4):
                    nc.gpsimd.tensor_tensor(x1_f[:, n, :], f(x_hi[:, 4 * c + n, :]), f(x_lo[:, 4 * c + n, :]),
                                            ALU.add).then_inc(x1_f_ready, 1)

            pool.wait_ge(diag_ready, 2)
            nc.gpsimd.memset(keep[:, :], 1.0).then_inc(o_lo_ready, 1)
            nc.gpsimd.memset(masked[:, :], 0.0).then_inc(mask_made, 1)
            nc.gpsimd.memset(seen[:, :], 1.0).then_inc(mask_made, 1)
            pool.wait_ge(mask_made, 2)
            below_diagonal(masked[:, S - P:S], 1.0)
            below_diagonal(seen[:, :], 0.0).then_inc(mask_made, 1)
            pool.wait_ge(mask_made, 3)
            x1_parts(0)
            with pool.Fori(0, PAIRS) as p:
                for dst, src, c in ((q_lo, q_hi, 0), (k_lo, k_hi, 2)):
                    for m in range(2):
                        pool.wait_ge(qk_hi_ready, p * 4 + (c + m + 1))
                        nc.gpsimd.tensor_tensor(dst[:, m, :], kf[:, m, :], f(src[:, m, :]),
                                                ALU.subtract).then_inc(qk_lo_ready, 1)
                for h in range(2):
                    for idx, i in enumerate(I_ORDER):
                        pool.wait_ge(sig_ready, p * 16 + (8 * h + 2 * idx + 2))
                        diagonal = wgt[:, W_OFF[i] + P * i:W_OFF[i] + P * i + P]
                        nc.gpsimd.tensor_tensor(diagonal, diagonal, seen[:, :], ALU.mult).then_inc(wgt_masked, 1)
                for h in range(2):
                    pool.wait_ge(o_hi_ready, p * 2 + (h + 1))
                    nc.gpsimd.tensor_tensor(o_lo[:, bass.ds(p * 2 + h, 1), :], kf[:, h:h + 1, :],
                                            f(o_hi[:, bass.ds(p * 2 + h, 1), :]),
                                            ALU.subtract).then_inc(o_lo_ready, 1)
            for c in range(1, 4):
                x1_parts(c)


_INS = ["x", "a_norm", "a_w_in", "a_conv_w", "a_conv_b", "a_w_r", "a_b_r", "a_w_i", "a_b_i", "a_lambda",
        "a_w_out", "kv_norm", "w_kv", "b_norm", "b_w_in", "b_w_out", "final_norm"]


def kernel(**inputs):
    import numpy as _np
    import concourse.bacc as _bacc
    from concourse import mybir as _mybir
    from concourse.bass_utils import run_bass_kernel_spmd as _run

    nc = _bacc.Bacc("TRN2", target_bir_lowering=False, num_devices=1, dynamic_dma_scratch_size=1024)
    f32 = _mybir.dt.float32
    arrays, args = {}, []
    for name in _INS:
        a = _np.ascontiguousarray(inputs[name])
        arrays[f"in_{name}"] = a
        args.append(nc.dram_tensor(f"in_{name}", a.shape, _mybir.dt.from_np(a.dtype), kind="ExternalInput").ap())
    args.append(nc.dram_tensor("out_0", (1, S, D), f32, kind="ExternalOutput").ap())
    build(nc, *args)
    r = _run(nc, [arrays], core_ids=[0])
    return r.results[0]["out_0"]
```
